# Optimizing a Trainium2 kernel written in Bass

```python
import math
import jax, jax.numpy as jnp
from jax import lax
import numpy as np

D_MODEL = 1024
BATCH = 1
SEQ = 256
DEPTH = 2

N_MIXERS = 4
D_FF = 2816
N_MOD = 9
EPS = 1e-6
Q_BLOCK = 128
GRID_W = 64

POOL_WINDOWS = (2, 4, 8, 16)
N_POOL = len(POOL_WINDOWS)
POOL_GROUP = D_MODEL // N_POOL

DIFF_HEADS = 8
DIFF_HEAD_DIM = D_MODEL // DIFF_HEADS // 2
DIFF_V_DIM = 2 * DIFF_HEAD_DIM
ROPE_THETA = 500000.0
ROT_DIM = DIFF_HEAD_DIM // 4

GQA_HEADS = 8
GQA_KV_HEADS = 2
GQA_HEAD_DIM = D_MODEL // GQA_HEADS
GQA_GROUP = GQA_HEADS // GQA_KV_HEADS
GQA_Q_DIM = GQA_HEADS * GQA_HEAD_DIM
GQA_KV_DIM = GQA_KV_HEADS * GQA_HEAD_DIM
AXIAL_THETA = 10000.0
AXIAL_DIM = GQA_HEAD_DIM // 2

CONV_WIDTH = 3


def rms_norm(x, g):
    xf = x.astype(jnp.float32)
    y = xf * lax.rsqrt(jnp.mean(xf * xf, axis=-1, keepdims=True) + EPS)
    return (y * g.astype(jnp.float32)).astype(x.dtype)

def modulate(h, shift, scale):
    return h * (1 + scale) + shift

def swiglu(h, w_gu, w_down):
    g, u = jnp.split(h @ w_gu, 2, axis=-1)
    return (jax.nn.silu(g) * u) @ w_down

def rope_tables(pos, dim, theta):
    inv = 1.0 / (theta ** (jnp.arange(0, dim, 2, dtype=jnp.float32) / dim))
    ang = pos.astype(jnp.float32)[:, None] * inv[None, :]
    return jnp.cos(ang), jnp.sin(ang)

def rope(x, cos, sin):
    half = x.shape[-1] // 2
    xf = x.astype(jnp.float32)
    x1, x2 = xf[..., :half], xf[..., half:]
    c = cos[None, :, None, :]
    s = sin[None, :, None, :]
    return jnp.concatenate([x1 * c - x2 * s, x2 * c + x1 * s], axis=-1).astype(x.dtype)

def sweep_query_blocks(fn, q):
    b, s = q.shape[:2]
    nblk = s // Q_BLOCK
    qb = jnp.moveaxis(q.reshape((b, nblk, Q_BLOCK) + q.shape[2:]), 1, 0)
    out = jnp.moveaxis(lax.map(fn, qb), 0, 1)
    return out.reshape((b, s) + out.shape[3:])

def pool_mixer(h, pool_w, pool_scale):
    b, s, d = h.shape
    cs = jnp.concatenate([jnp.zeros((b, 1, d), jnp.float32),
                          jnp.cumsum(h.astype(jnp.float32), axis=1)], axis=1)
    t = jnp.arange(s)
    diffs = []
    for g, win in enumerate(POOL_WINDOWS):
        lo = jnp.clip(t - win // 2, 0, s)
        hi = jnp.clip(t + win // 2, 0, s)
        csg = cs[..., g * POOL_GROUP:(g + 1) * POOL_GROUP]
        mean = (jnp.take(csg, hi, axis=1) - jnp.take(csg, lo, axis=1)) / (hi - lo).astype(jnp.float32)[None, :, None]
        diffs.append(mean.astype(h.dtype) - h[..., g * POOL_GROUP:(g + 1) * POOL_GROUP])
    dgrp = jnp.stack(diffs, axis=2)
    y = jnp.einsum('bsgc,gce->bsge', dgrp, pool_w).reshape(b, s, d)
    return y * pool_scale

def diff_attention(h, w_qkv, lam, subln_g, w_o, cos, sin, layer_idx):
    b, s, d = h.shape
    q, k, v = jnp.split(h @ w_qkv, 3, axis=-1)
    q = q.reshape(b, s, 2 * DIFF_HEADS, DIFF_HEAD_DIM)
    k = k.reshape(b, s, 2 * DIFF_HEADS, DIFF_HEAD_DIM)
    v = v.reshape(b, s, DIFF_HEADS, DIFF_V_DIM)
    q = jnp.concatenate([rope(q[..., :ROT_DIM], cos, sin), q[..., ROT_DIM:]], axis=-1)
    k = jnp.concatenate([rope(k[..., :ROT_DIM], cos, sin), k[..., ROT_DIM:]], axis=-1)
    q = (q * DIFF_HEAD_DIM ** -0.5).reshape(b, s, DIFF_HEADS, 2, DIFF_HEAD_DIM)
    k = k.reshape(b, s, DIFF_HEADS, 2, DIFF_HEAD_DIM)
    lam_init = 0.8 - 0.6 * math.exp(-0.3 * layer_idx)
    lf = lam.astype(jnp.float32)
    lam_full = jnp.exp(jnp.sum(lf[0] * lf[1])) - jnp.exp(jnp.sum(lf[2] * lf[3])) + lam_init

    def block(qb):
        sc = jnp.einsum('bqhcd,bkhcd->bhcqk', qb, k, preferred_element_type=jnp.float32)
        p = jax.nn.softmax(sc, axis=-1)
        a = p[:, :, 0] - lam_full * p[:, :, 1]
        return jnp.einsum('bhqk,bkhe->bqhe', a.astype(v.dtype), v)

    o = sweep_query_blocks(block, q)
    o = rms_norm(o, subln_g) * (1 - lam_init)
    return o.reshape(b, s, d) @ w_o

def gqa_axial_attention(h, w_qkv, q_norm_g, k_norm_g, w_o, cos_r, sin_r, cos_c, sin_c):
    b, s, d = h.shape
    qkv = h @ w_qkv
    q = qkv[..., :GQA_Q_DIM].reshape(b, s, GQA_HEADS, GQA_HEAD_DIM)
    k = qkv[..., GQA_Q_DIM:GQA_Q_DIM + GQA_KV_DIM].reshape(b, s, GQA_KV_HEADS, GQA_HEAD_DIM)
    v = qkv[..., GQA_Q_DIM + GQA_KV_DIM:].reshape(b, s, GQA_KV_HEADS, GQA_HEAD_DIM)
    q = rms_norm(q, q_norm_g)
    k = rms_norm(k, k_norm_g)

    def axial(t):
        return jnp.concatenate([rope(t[..., :AXIAL_DIM], cos_r, sin_r),
                                rope(t[..., AXIAL_DIM:], cos_c, sin_c)], axis=-1)

    q = (axial(q) * GQA_HEAD_DIM ** -0.5).reshape(b, s, GQA_KV_HEADS, GQA_GROUP, GQA_HEAD_DIM)
    k = axial(k)

    def block(qb):
        sc = jnp.einsum('bqgrd,bkgd->bgrqk', qb, k, preferred_element_type=jnp.float32)
        p = jax.nn.softmax(sc, axis=-1)
        return jnp.einsum('bgrqk,bkgd->bqgrd', p.astype(v.dtype), v)

    o = sweep_query_blocks(block, q)
    return o.reshape(b, s, d) @ w_o

def short_conv_mixer(h, w_in, w_conv, w_out):
    d = h.shape[-1]
    gb, gc, u = jnp.split(h @ w_in, 3, axis=-1)
    z = gc * u
    zc = lax.conv_general_dilated(z, w_conv[:, None, :], window_strides=(1,),
                                  padding=[((CONV_WIDTH - 1) // 2, (CONV_WIDTH - 1) // 2)],
                                  dimension_numbers=('NWC', 'WIO', 'NWC'),
                                  feature_group_count=d)
    return (gb * zc) @ w_out

def first_inputs(seed: int = 0) -> dict:
    key = jax.random.key(seed)
    ks = jax.random.split(key, 24)

    def nrm(k, shape, scale):
        return jax.random.normal(k, shape, jnp.float32) * scale

    D = D_MODEL
    return {
        "x": nrm(ks[0], (BATCH, SEQ, D), 1.0),
        "c": nrm(ks[1], (BATCH, D), 1.0),
        "mod_w": nrm(ks[2], (DEPTH, D, N_MOD * D), 0.5 * D ** -0.5),
        "mod_b": nrm(ks[3], (DEPTH, N_MOD * D), 0.02),
        "norm_g": 1.0 + nrm(ks[4], (DEPTH, 3, D), 0.1),
        "ffn_w_gu": nrm(ks[5], (DEPTH, 2, D, 2 * D_FF), D ** -0.5),
        "ffn_w_down": nrm(ks[6], (DEPTH, 2, D_FF, D), D_FF ** -0.5),
        "pool_w": nrm(ks[7], (N_POOL, POOL_GROUP, POOL_GROUP), POOL_GROUP ** -0.5),
        "pool_scale": 1.0 + nrm(ks[8], (D,), 0.1),
        "diff_w_qkv": nrm(ks[9], (D, 3 * D), D ** -0.5),
        "diff_lambda": nrm(ks[10], (4, DIFF_HEAD_DIM), 0.1),
        "diff_subln_g": 1.0 + nrm(ks[11], (DIFF_V_DIM,), 0.1),
        "diff_w_o": nrm(ks[12], (D, D), D ** -0.5),
        "gqa_w_qkv": nrm(ks[13], (D, GQA_Q_DIM + 2 * GQA_KV_DIM), D ** -0.5),
        "gqa_q_norm_g": 1.0 + nrm(ks[14], (GQA_HEAD_DIM,), 0.1),
        "gqa_k_norm_g": 1.0 + nrm(ks[15], (GQA_HEAD_DIM,), 0.1),
        "gqa_w_o": nrm(ks[16], (D, D), D ** -0.5),
        "conv_w_in": nrm(ks[17], (D, 3 * D), D ** -0.5),
        "conv_w": nrm(ks[18], (CONV_WIDTH, D), CONV_WIDTH ** -0.5),
        "conv_w_out": nrm(ks[19], (D, D), D ** -0.5),
        "final_g": 1.0 + nrm(ks[20], (D,), 0.1),
    }

def first_block(x, c, mod_w, mod_b, norm_g, ffn_w_gu, ffn_w_down, pool_w, pool_scale,
              diff_w_qkv, diff_lambda, diff_subln_g, diff_w_o,
              gqa_w_qkv, gqa_q_norm_g, gqa_k_norm_g, gqa_w_o,
              conv_w_in, conv_w, conv_w_out, final_g):
    s = x.shape[1]
    t = jnp.arange(s)
    cos1, sin1 = rope_tables(t, ROT_DIM, ROPE_THETA)
    rows = s // GRID_W
    row_pos = jnp.broadcast_to(jnp.arange(rows)[:, None], (rows, GRID_W)).reshape(-1)
    col_pos = jnp.broadcast_to(jnp.arange(GRID_W)[None, :], (rows, GRID_W)).reshape(-1)
    cos_r, sin_r = rope_tables(row_pos, AXIAL_DIM, AXIAL_THETA)
    cos_c, sin_c = rope_tables(col_pos, AXIAL_DIM, AXIAL_THETA)

    c_act = jax.nn.silu(c)
    for i in range(DEPTH):
        mod = (c_act @ mod_w[i] + mod_b[i])[:, None, :]
        sh0, sc0, g0, sh1, sc1, g1, sh2, sc2, g2 = jnp.split(mod, N_MOD, axis=-1)

        h = modulate(rms_norm(x, norm_g[i, 0]), sh0, sc0)
        x = x + 0.5 * g0 * swiglu(h, ffn_w_gu[i, 0], ffn_w_down[i, 0])

        h = modulate(rms_norm(x, norm_g[i, 1]), sh1, sc1)
        kind = i % N_MIXERS
        if kind == 0:
            y = pool_mixer(h, pool_w, pool_scale)
        elif kind == 1:
            y = diff_attention(h, diff_w_qkv, diff_lambda, diff_subln_g, diff_w_o, cos1, sin1, i)
        elif kind == 2:
            y = gqa_axial_attention(h, gqa_w_qkv, gqa_q_norm_g, gqa_k_norm_g, gqa_w_o,
                                    cos_r, sin_r, cos_c, sin_c)
        else:
            y = short_conv_mixer(h, conv_w_in, conv_w, conv_w_out)
        x = x + g1 * y

        h = modulate(rms_norm(x, norm_g[i, 2]), sh2, sc2)
        x = x + 0.5 * g2 * swiglu(h, ffn_w_gu[i, 1], ffn_w_down[i, 1])

    return rms_norm(x, final_g)


DEPTH_2 = 1

A_HEADS = 8
A_HEAD_DIM = 64
A_WIDTH = A_HEADS * A_HEAD_DIM
MOBA_BLOCK = 256
MOBA_TOPK = 3
MOBA_QCHUNK = 32
ROPE_THETA_2 = 10000.0
B_HEADS = 4
B_HEAD_DIM = 128
B_WIDTH = B_HEADS * B_HEAD_DIM
MLSTM_CHUNK = 64
CONV_WIDTH_2 = 4
D_FF_2 = ((8 * D_MODEL + 3 * 256 - 1) // (3 * 256)) * 256
NORM_EPS = 1e-6

IN_SIZES = [A_WIDTH, A_WIDTH, A_WIDTH,
            2 * B_WIDTH,
            B_WIDTH, B_WIDTH,
            B_HEADS, B_HEADS,
            D_MODEL, D_MODEL]
IN_WIDTH = sum(IN_SIZES)
IN_SPLITS = [int(s) for s in np.cumsum(IN_SIZES)[:-1]]


def rms_norm_2(x, g):
    xf = x.astype(jnp.float32)
    y = xf * lax.rsqrt(jnp.mean(xf * xf, axis=-1, keepdims=True) + NORM_EPS)
    return (y * g.astype(jnp.float32)).astype(x.dtype)

def rope_2(x, pos):
    half = x.shape[-1] // 2
    inv = ROPE_THETA_2 ** (-jnp.arange(half, dtype=jnp.float32) / half)
    ang = pos.astype(jnp.float32)[:, None] * inv[None, :]
    cos, sin = jnp.cos(ang), jnp.sin(ang)
    xf = x.astype(jnp.float32)
    x1, x2 = xf[..., :half], xf[..., half:]
    return jnp.concatenate([x1 * cos - x2 * sin, x2 * cos + x1 * sin], axis=-1).astype(x.dtype)

def causal_depthwise_conv(x, w):
    width, chans = w.shape
    return lax.conv_general_dilated(
        x, w[:, None, :].astype(x.dtype), window_strides=(1,),
        padding=((width - 1, 0),), dimension_numbers=('NWC', 'WIO', 'NWC'),
        feature_group_count=chans)

def moba_attention(q, k, v):
    bn, nh, s, dh = q.shape
    nb = -(-s // MOBA_BLOCK)
    sp = nb * MOBA_BLOCK
    pad = ((0, 0), (0, 0), (0, sp - s), (0, 0))
    q, k, v = jnp.pad(q, pad), jnp.pad(k, pad), jnp.pad(v, pad)
    kb = k.reshape(bn, nh, nb, MOBA_BLOCK, dh)
    vb = v.reshape(bn, nh, nb, MOBA_BLOCK, dh)
    scale = dh ** -0.5
    topk = min(MOBA_TOPK, nb - 1)
    nq = sp // MOBA_QCHUNK
    qc = jnp.moveaxis(q.reshape(bn, nh, nq, MOBA_QCHUNK, dh), 2, 0)
    starts = jnp.arange(nq) * MOBA_QCHUNK
    if topk > 0:
        kmean = kb.astype(jnp.float32).mean(axis=3)
        gate = jnp.einsum('bhsd,bhnd->bhsn', q.astype(jnp.float32), kmean)
        q_blk = jnp.arange(sp) // MOBA_BLOCK
        past = jnp.arange(nb)[None, :] < q_blk[:, None]
        gate = jnp.where(past, gate, -jnp.inf)
        top_val, top_idx = lax.top_k(gate, topk)
        valid = jnp.isfinite(top_val)
        idx_c = jnp.moveaxis(top_idx.reshape(bn, nh, nq, MOBA_QCHUNK, topk), 2, 0)
        val_c = jnp.moveaxis(valid.reshape(bn, nh, nq, MOBA_QCHUNK, topk), 2, 0)
        xs = (qc, starts, idx_c, val_c)
    else:
        xs = (qc, starts)
    bi = jnp.arange(bn)[:, None, None, None]
    hi = jnp.arange(nh)[None, :, None, None]

    def attend_chunk(args):
        qi, start = args[0], args[1]
        blk = start // MOBA_BLOCK
        k_own = lax.dynamic_index_in_dim(kb, blk, axis=2, keepdims=False)
        v_own = lax.dynamic_index_in_dim(vb, blk, axis=2, keepdims=False)
        qpos = start + jnp.arange(MOBA_QCHUNK)
        kpos = blk * MOBA_BLOCK + jnp.arange(MOBA_BLOCK)
        causal = kpos[None, :] <= qpos[:, None]
        s_own = jnp.einsum('bhqd,bhkd->bhqk', qi, k_own).astype(jnp.float32) * scale
        s_own = jnp.where(causal, s_own, -jnp.inf)
        if topk > 0:
            idx_i, valid_i = args[2], args[3]
            k_sel = kb[bi, hi, idx_i]
            v_sel = vb[bi, hi, idx_i]
            s_sel = jnp.einsum('bhqd,bhqrkd->bhqrk', qi, k_sel).astype(jnp.float32) * scale
            s_sel = jnp.where(valid_i[..., None], s_sel, -jnp.inf)
            s_sel = s_sel.reshape(bn, nh, MOBA_QCHUNK, topk * MOBA_BLOCK)
            p = jax.nn.softmax(jnp.concatenate([s_sel, s_own], axis=-1), axis=-1).astype(v.dtype)
            p_sel = p[..., :topk * MOBA_BLOCK].reshape(bn, nh, MOBA_QCHUNK, topk, MOBA_BLOCK)
            return (jnp.einsum('bhqrk,bhqrkd->bhqd', p_sel, v_sel)
                    + jnp.einsum('bhqk,bhkd->bhqd', p[..., topk * MOBA_BLOCK:], v_own))
        p = jax.nn.softmax(s_own, axis=-1).astype(v.dtype)
        return jnp.einsum('bhqk,bhkd->bhqd', p, v_own)

    out = lax.map(attend_chunk, xs)
    return jnp.moveaxis(out, 0, 2).reshape(bn, nh, sp, dh)[:, :, :s]

def mlstm_chunkwise(q, k, v, i_pre, f_pre):
    bn, nh, s, d = q.shape
    L = MLSTM_CHUNK
    nc = s // L
    f32 = jnp.float32
    q = q.astype(f32)
    k = k.astype(f32) * (d ** -0.5)
    v = v.astype(f32)
    log_f = jax.nn.log_sigmoid(f_pre.astype(f32))
    log_i = i_pre.astype(f32)

    def chunks(a):
        return jnp.moveaxis(a.reshape(bn, nh, nc, L, *a.shape[3:]), 2, 0)

    tri = jnp.tril(jnp.ones((L, L), dtype=bool))

    def step(carry, xs):
        C, n, m = carry
        qc, kc, vc, ic, fc = xs
        b = jnp.cumsum(fc, axis=-1)
        dmat = jnp.where(tri, b[..., :, None] - b[..., None, :] + ic[..., None, :], -jnp.inf)
        m_inter = b + m[..., None]
        m_t = jnp.maximum(m_inter, dmat.max(axis=-1))
        sc = jnp.einsum('bhtd,bhsd->bhts', qc, kc) * jnp.exp(dmat - m_t[..., None])
        w_inter = jnp.exp(m_inter - m_t)
        num = (jnp.einsum('bhts,bhse->bhte', sc, vc)
               + w_inter[..., None] * jnp.einsum('bhtd,bhde->bhte', qc, C))
        den = sc.sum(axis=-1) + w_inter * jnp.einsum('bhtd,bhd->bht', qc, n)
        h = num / jnp.maximum(jnp.abs(den), jnp.exp(-m_t))[..., None]
        b_tot = b[..., -1]
        g = b_tot[..., None] - b + ic
        m_new = jnp.maximum(b_tot + m, g.max(axis=-1))
        w_c = jnp.exp(b_tot + m - m_new)
        w_s = jnp.exp(g - m_new[..., None])
        C = w_c[..., None, None] * C + jnp.einsum('bhs,bhsd,bhse->bhde', w_s, kc, vc)
        n = w_c[..., None] * n + jnp.einsum('bhs,bhsd->bhd', w_s, kc)
        return (C, n, m_new), h

    init = (jnp.zeros((bn, nh, d, d), f32), jnp.zeros((bn, nh, d), f32), jnp.zeros((bn, nh), f32))
    _, hs = lax.scan(step, init, (chunks(q), chunks(k), chunks(v), chunks(log_i), chunks(log_f)))
    return jnp.moveaxis(hs, 0, 2).reshape(bn, nh, s, d)

def second_inputs(seed: int = 0) -> dict:
    key = jax.random.key(seed)
    ks = jax.random.split(key, 16)
    nrm = jax.random.normal
    f32 = jnp.float32
    return {
        "x": nrm(ks[0], (BATCH, SEQ, D_MODEL), f32),
        "norm_mix_g": 1.0 + 0.02 * nrm(ks[1], (DEPTH_2, D_MODEL), f32),
        "w_in": nrm(ks[2], (DEPTH_2, D_MODEL, IN_WIDTH), f32) * D_MODEL ** -0.5,
        "conv_w": nrm(ks[3], (DEPTH_2, CONV_WIDTH_2, 2 * B_WIDTH), f32) * CONV_WIDTH_2 ** -0.5,
        "b_igate": 0.1 * nrm(ks[4], (DEPTH_2, B_HEADS), f32),
        "b_fgate": jnp.linspace(3.0, 6.0, B_HEADS, dtype=f32)[None, :] + 0.1 * nrm(ks[5], (DEPTH_2, B_HEADS), f32),
        "mlstm_norm_g": 1.0 + 0.02 * nrm(ks[6], (DEPTH_2, B_WIDTH), f32),
        "w_proj_a": nrm(ks[7], (DEPTH_2, A_WIDTH, D_MODEL), f32) * A_WIDTH ** -0.5,
        "w_proj_b": nrm(ks[8], (DEPTH_2, B_WIDTH, D_MODEL), f32) * B_WIDTH ** -0.5,
        "w_out": nrm(ks[9], (DEPTH_2, D_MODEL, D_MODEL), f32) * D_MODEL ** -0.5,
        "norm_ffn_g": 1.0 + 0.02 * nrm(ks[10], (DEPTH_2, D_MODEL), f32),
        "w_gate_up": nrm(ks[11], (DEPTH_2, D_MODEL, 2 * D_FF_2), f32) * D_MODEL ** -0.5,
        "w_down": nrm(ks[12], (DEPTH_2, D_FF_2, D_MODEL), f32) * D_FF_2 ** -0.5,
        "norm_final_g": 1.0 + 0.02 * nrm(ks[13], (D_MODEL,), f32),
    }

def second_block(x, norm_mix_g, w_in, conv_w, b_igate, b_fgate, mlstm_norm_g, w_proj_a, w_proj_b,
              w_out, norm_ffn_g, w_gate_up, w_down, norm_final_g):
    bn, s, _ = x.shape
    pos = jnp.arange(s)

    def to_heads(t, nh):
        return t.reshape(bn, s, nh, -1).transpose(0, 2, 1, 3)

    h = x
    for l in range(DEPTH_2):
        u = rms_norm_2(h, norm_mix_g[l])
        z = u @ w_in[l]
        qa, ka, va, qk_b, vb, ob, ib, fb, ga, gb = jnp.split(z, IN_SPLITS, axis=-1)

        qa = rope_2(to_heads(qa, A_HEADS), pos)
        ka = rope_2(to_heads(ka, A_HEADS), pos)
        ya = moba_attention(qa, ka, to_heads(va, A_HEADS))
        ya = ya.transpose(0, 2, 1, 3).reshape(bn, s, A_WIDTH)

        qk_b = jax.nn.silu(causal_depthwise_conv(qk_b, conv_w[l]))
        qb, kb_ = jnp.split(qk_b, 2, axis=-1)
        i_pre = (ib + b_igate[l].astype(ib.dtype)).transpose(0, 2, 1)
        f_pre = (fb + b_fgate[l].astype(fb.dtype)).transpose(0, 2, 1)
        hb = mlstm_chunkwise(to_heads(qb, B_HEADS), to_heads(kb_, B_HEADS), to_heads(vb, B_HEADS),
                             i_pre, f_pre)
        hb = hb * lax.rsqrt(jnp.mean(hb * hb, axis=-1, keepdims=True) + NORM_EPS)
        hb = hb.transpose(0, 2, 1, 3).reshape(bn, s, B_WIDTH) * mlstm_norm_g[l].astype(jnp.float32)
        yb = (jax.nn.sigmoid(ob.astype(jnp.float32)) * hb).astype(u.dtype)

        merged = (jax.nn.sigmoid(ga) * (ya @ w_proj_a[l])
                  + jax.nn.sigmoid(gb) * (yb @ w_proj_b[l]))
        h = h + merged @ w_out[l]

        u = rms_norm_2(h, norm_ffn_g[l])
        g, up = jnp.split(u @ w_gate_up[l], 2, axis=-1)
        h = h + (jax.nn.silu(g) * up) @ w_down[l]

    return rms_norm_2(h, norm_final_g)


def setup_inputs(seed=0):
    out = dict(first_inputs(seed))
    for name, value in second_inputs(seed + 1).items():
        if name != "x":
            out[name + "_2"] = value
    return out


def reference(
    x, c, mod_w, mod_b, norm_g, ffn_w_gu, ffn_w_down, pool_w, pool_scale, diff_w_qkv,
    diff_lambda, diff_subln_g, diff_w_o, gqa_w_qkv, gqa_q_norm_g, gqa_k_norm_g, gqa_w_o,
    conv_w_in, conv_w, conv_w_out, final_g, norm_mix_g_2, w_in_2, conv_w_2, b_igate_2,
    b_fgate_2, mlstm_norm_g_2, w_proj_a_2, w_proj_b_2, w_out_2, norm_ffn_g_2, w_gate_up_2,
    w_down_2, norm_final_g_2,
):
    x = first_block(
        x, c, mod_w, mod_b, norm_g, ffn_w_gu, ffn_w_down, pool_w, pool_scale, diff_w_qkv,
        diff_lambda, diff_subln_g, diff_w_o, gqa_w_qkv, gqa_q_norm_g, gqa_k_norm_g, gqa_w_o,
        conv_w_in, conv_w, conv_w_out, final_g,
    )
    return second_block(
        x, norm_mix_g_2, w_in_2, conv_w_2, b_igate_2, b_fgate_2, mlstm_norm_g_2, w_proj_a_2,
        w_proj_b_2, w_out_2, norm_ffn_g_2, w_gate_up_2, w_down_2, norm_final_g_2,
    )


_drawn_inputs = setup_inputs


def setup_inputs(seed=0):
    import zlib

    import numpy as np

    out = dict(_drawn_inputs(seed))
    spreads = {}
    factors = {'norm_mix_g_2': 5.071,
     'b_igate_2': 200.0,
     'mlstm_norm_g_2': 23.625,
     'norm_ffn_g_2': 11.063,
     'norm_final_g_2': 21.585}
    for name, (base, spread) in spreads.items():
        noise = np.random.default_rng([zlib.crc32(name.encode()), seed]).standard_normal(out[name].shape)
        drawn = base * np.exp(spread * noise) if base else spread * noise
        out[name] = __import__('jax').numpy.asarray(drawn.astype(out[name].dtype))
    for name, factor in factors.items():
        out[name] = (out[name] * factor).astype(out[name].dtype)
    return out
```

```python
import math
from collections import namedtuple
from contextlib import ExitStack

import numpy as np

import concourse.bass as bass
from concourse import mybir

F32 = mybir.dt.float32
F32R = mybir.dt.float32r
ALU = mybir.AluOpType
ACT = mybir.ActivationFunctionType
AX = mybir.AxisListType

P = 128
D = 1024
S = 256
TB = S // P
KT = D // P
FF = 2816
EPS = 1e-6
PIECE = 2048
BLK = 512
FFW = 256
STEPS = FF // FFW
RAW = 3
RING = 6
NMOD = 9
MCH = 512
A, B, T, M = 4, 5, 6, 7
WINDOWS = (2, 4, 8, 16)
H1, HD1 = 8, 64
ROT = HD1 // 4
HA, HDA = 8, 64
HB, HDB = 4, 128
LAM_INIT = 0.8 - 0.6 * math.exp(-0.3 * 1)
IN_COLS = 5640
GATE_COL = 3584
HUGE = 1e30


class Nth:

    def __init__(self, first, i=None, per=0):
        self.first, self.i, self.per = first, i, per
        self.at = first if i is None else i * per + first

    def back(self, k):
        return self.first - k if self.i is None else self.i * self.per + (self.first - k)

    def lap(self, size):
        n = self.first // size
        return n if self.i is None else self.i * (self.per // size) + n


class Tally:

    def __init__(self):
        self.n, self.i, self.per, self.start = {}, None, {}, {}

    def next(self, name):
        n = self.n.get(name, 0)
        self.n[name] = n + 1
        if self.i is None:
            return Nth(n)
        return Nth(n, self.i, self.per[name])

    def seen(self, name):
        n = self.n.get(name, 0)
        return n if self.i is None else self.i * self.per[name] + n

    def enter(self, i, per):
        self.i, self.per, self.start = i, per, {k: self.n.get(k, 0) for k in per}

    def leave(self, turns):
        for k, per in self.per.items():
            assert self.n.get(k, 0) - self.start[k] == per, (k, per)
            self.n[k] = self.start[k] + per * turns
        self.i = None


def constants():
    f = np.float32
    t = np.arange(S, dtype=f)
    inv1 = (f(1.0) / (f(500000.0) ** (np.arange(0, ROT, 2, dtype=f) / f(ROT)))).astype(f)
    ang1 = (t[:, None] * inv1[None, :]).astype(f)
    half = HDA // 2
    inv2 = (f(10000.0) ** (-np.arange(half, dtype=f) / f(half))).astype(f)
    ang2 = (t[:, None] * inv2[None, :]).astype(f)

    def rows(a):
        return a.reshape(TB, P, -1).transpose(1, 0, 2)

    rope1 = np.stack([rows(np.cos(ang1)), rows(np.sin(ang1))], 1).astype(f)
    rope2 = np.stack([rows(np.cos(ang2)), rows(np.sin(ang2))], 1).astype(f)
    edge = np.ones((4, 2, 8), f)
    for g, w in enumerate(WINDOWS):
        for j in range(8):
            for side, tok in ((0, j), (1, S - 8 + j)):
                n = min(tok + w // 2, S) - max(tok - w // 2, 0)
                edge[g, side, j] = f(w) / f(n)
    q, k = np.arange(P)[:, None], np.arange(P)[None, :]
    mask_q = np.where(k <= q, 0.0, -HUGE).astype(f)
    mask_k = np.where(q <= k, 0.0, HUGE).astype(f)
    pick = np.zeros((4, 4, P), f)
    for h in range(4):
        pick[h, h] = 1.0
    return {
        "ident": np.eye(P, dtype=f),
        "rope1": rope1.reshape(P, -1), "rope2": rope2.reshape(P, -1),
        "edge": np.broadcast_to(edge.reshape(1, -1), (P, 64)).copy(),
        "mask_q": mask_q, "mask_k": mask_k, "pick": pick.reshape(4, 4 * P),
    }


INPUTS = ["x", "c", "mod_w", "mod_b", "norm_g", "ffn_w_gu", "ffn_w_down", "pool_w", "pool_scale",
          "diff_w_qkv", "diff_lambda", "diff_subln_g", "diff_w_o", "final_g", "norm_mix_g_2",
          "w_in_2", "conv_w_2", "b_igate_2", "b_fgate_2", "mlstm_norm_g_2", "w_proj_a_2",
          "w_proj_b_2", "w_out_2", "norm_ffn_g_2", "w_gate_up_2", "w_down_2", "norm_final_g_2"]


def build(nc, d, out):
    ctx = ExitStack()

    def sb(name, cols, dt=F32, parts=P):
        return ctx.enter_context(nc.sbuf_tensor(name, [parts, cols], dt))

    def sem(name):
        return ctx.enter_context(nc.semaphore(name))

    with ctx:
        ps = ctx.enter_context(nc.psum_tensor("ps", [P, 8, BLK], F32))
        raw = sb("raw", RAW * PIECE)
        whi = sb("whi", RING * PIECE, F32R)
        wlo = sb("wlo", RING * PIECE, F32R)
        xres = sb("xres", TB * D)
        nthi = sb("nthi", KT * S, F32R)
        ntlo = sb("ntlo", KT * S, F32R)
        xn = sb("xn", TB * D)
        gate = sb("gate", D)
        hthi = sb("hthi", 2 * 2 * S, F32R)
        htlo = sb("htlo", 2 * 2 * S, F32R)
        arena = sb("arena", 9984)
        ident = sb("ident", P)
        ones = sb("ones", P)
        cols = sb("cols", 104)
        modb = sb("modb", 2 * NMOD * KT)
        modc = sb("modc", 2 * NMOD * KT)
        scol = sb("scol", KT)
        cact = sb("cact", KT)
        ss = sb("ss", 2)
        rstd = sb("rstd", 2)
        power = sb("power", 2)
        small = sb("small", 96)

        x = xres[:, :].rearrange("p (t n) -> p t n", t=TB)
        xnt = xn[:, :].rearrange("p (t n) -> p t n", t=TB)
        nth = nthi[:, :].rearrange("p (k s) -> p k s", k=KT)
        ntl = ntlo[:, :].rearrange("p (k s) -> p k s", k=KT)
        hth = hthi[:, :].rearrange("p (b k s) -> p b k s", b=2, k=2)
        htl = htlo[:, :].rearrange("p (b k s) -> p b k s", b=2, k=2)
        C_NORM, C_C, C_MIX, C_FFN, C_CONV = 0, 48, 56, 64, 72
        NROWS = 104

        def norm_col(layer, j):
            at = C_NORM + (3 * layer + j) * KT
            return cols[:, at:at + KT]

        def mod_cols(layer, v):
            at = (layer * NMOD + v) * KT
            return modc[:, at:at + KT]

        class Arena:

            def __init__(self):
                self.at = 0

            def take(self, n, parts=P):
                self.at += n
                assert self.at <= 9984, self.at
                return arena[0:parts, self.at - n:self.at]

        ar = Arena()
        mraw = [ar.take(4 * MCH).rearrange("p (k n) -> p k n", k=4) for _ in range(2)]
        acc = ar.take(MCH)
        sil = ar.take(TB * FFW).rearrange("p (t n) -> p t n", t=TB)
        prow = ar.take(P)
        brow = [ar.take(P, 72) for _ in range(2)]

        row = arena[:, 9984 - D:9984]
        ar = Arena()
        ar.at = 4 * MCH * 2 + MCH + TB * FFW
        padded = ar.take(2 * (S + 16)).rearrange("p (k s) -> p k s", k=2)
        win = [ar.take(2 * (S + 16)).rearrange("p (k s) -> p k s", k=2) for _ in range(2)]
        edge = ar.take(64).rearrange("p (g e j) -> p g e j", g=4, e=2)
        ar = Arena()
        qkv = ar.take(TB * 3 * D).rearrange("p (t n) -> p t n", t=TB)
        qkT = ar.take(2 * BLK).rearrange("p (b n) -> p b n", b=2)
        pr = ar.take(2 * BLK).rearrange("p (c t k) -> p c t k", c=2, t=2)
        av = ar.take(BLK).rearrange("p (t k) -> p t k", t=2)
        avT = ar.take(BLK).rearrange("p (t k q) -> p t k q", t=2, k=2)
        subln = ar.take(P)
        rope1 = ar.take(32).rearrange("p (c t j) -> p c t j", c=2, t=2)
        lamrow = ar.take(256)
        lamt = ar.take(128)
        ar = Arena()
        qkva = ar.take(TB * 1536).rearrange("p (t n) -> p t n", t=TB)
        vbx = ar.take(TB * 516).rearrange("p (t h n) -> p t h n", t=TB, h=4)
        obt = ar.take(TB * 512).rearrange("p (t n) -> p t n", t=TB)
        gab = ar.take(TB * 1536).rearrange("p (t n) -> p t n", t=TB)
        gab2 = gate[:, :].rearrange("p (t n) -> p t n", t=TB)
        w8 = ar.take(64).rearrange("p (k n) -> p k n", k=KT)
        rope2 = ar.take(128).rearrange("p (c t j) -> p c t j", c=2, t=2)
        rest = ar.at
        convin = ar.take(TB * 512).rearrange("p (t n) -> p t n", t=TB)
        convT = ar.take(2 * 259).rearrange("p (b n) -> p b n", b=2)
        ar.at = rest
        qkTa = ar.take(BLK)
        pa = ar.take(384)
        paT = ar.take(384)
        ar.at = rest
        decay = ar.take(384)
        scT = ar.take(384)
        pick = ar.take(4 * P, 4)
        junkh = ar.take(P)
        va_rows = [qkva[0:4, t, 1024 + 256 * i:1280 + 256 * i] for t in range(2) for i in range(2)]

        qkc = xn[:, :].rearrange("p (k s) -> p k s", k=KT)
        diag = xn[:, 0:D].rearrange("p (k n) -> p k n", k=KT)
        mask_q, mask_k = modb[:, 0:P], modc[:, 0:P]
        gz = small[:, 0:16].rearrange("p (t g) -> p t g", t=TB)
        gbias = small[:, 16:24]
        agate = small[:, 24:40].rearrange("p (g t h) -> p g t h", g=2, t=TB)
        lam = small[:, 0:8]
        top, total, inv, invl = (small[:, 40 + 4 * i:44 + 4 * i] for i in range(4))
        hss = small[:, 56:72]

        raw_landed = [sem(f"raw_landed{i}") for i in range(RAW)]
        w_hi, w_lo, w_used = sem("w_hi"), sem("w_lo"), sem("w_used")
        filled = {b: sem(f"filled{b}") for b in (A, B, T, M)}
        drained = {b: sem(f"drained{b}") for b in (A, B, T, M)}
        sums_done = sem("sums_done")
        sums_read = [sem("sums_read0"), sem("sums_read1")]
        silu_done = sem("silu_done")
        h_ready = sem("h_ready")
        ht_hi, ht_lo = sem("ht_hi"), sem("ht_lo")
        mod_landed = [sem("mod_landed0"), sem("mod_landed1")]
        mod_read = [sem("mod_read0"), sem("mod_read1")]
        acc_step, acc_ready, acc_used, modc_ready = sem("acc_step"), sem("acc_ready"), sem("acc_used"), sem("modc_ready")
        diag_ready, gate_ready, gate_step = sem("diag_ready"), sem("gate_ready"), sem("gate_step")
        gate_used = sem("gate_used")
        x_ready, x_step, sq_done, rstd_v, rstd_done = sem("x_ready"), sem("x_step"), sem("sq_done"), sem("rstd_v"), sem("rstd_done")
        xn_ready, hf_ready, nt_hi, nt_lo = sem("xn_ready"), sem("hf_ready"), sem("nt_hi"), sem("nt_lo")
        x_landed, prm_landed, ident_landed = sem("x_landed"), sem("prm_landed"), sem("ident_landed")
        cols_copied = sem("cols_copied")
        row_landed, edge_landed, attn_landed, mix_landed, late_landed = (
            sem("row_landed"), sem("edge_landed"), sem("attn_landed"), sem("mix_landed"), sem("late_landed"))
        consts_set, cact_ready = sem("consts_set"), sem("cact_ready")
        out_done, y_ready = sem("out_done"), sem("y_ready")
        dve_chain, pool_chain, act_chain = sem("dve_chain"), sem("pool_chain"), sem("act_chain")
        pool_diff, pool_hi, pool_lo = sem("pool_diff"), sem("pool_hi"), sem("pool_lo")
        lam_prod, lam_exp = sem("lam_prod"), sem("lam_exp")
        roped = sem("roped")
        top_ready, probs_ready, mix_ready, head_out, out_copied = (
            sem("top_ready"), sem("probs_ready"), sem("mix_ready"), sem("head_out"), sem("out_copied"))
        heads_v, heads_rstd, heads_normed = sem("heads_v"), sem("heads_rstd"), sem("heads_normed")
        conv_in, conv_sum, conv_out, conv_done = sem("conv_in"), sem("conv_sum"), sem("conv_out"), sem("conv_done")
        gated = sem("gated")
        mask_landed, attention_over = sem("mask_landed"), sem("attention_over")
        rows_step, rows_act, rows_done = sem("rows_step"), sem("rows_act"), sem("rows_done")
        hb_ready, den_abs = sem("hb_ready"), sem("den_abs")
        den_ready, decay_in, decay_out = sem("den_ready"), sem("decay_in"), sem("decay_out")
        y_done, merged = sem("y_done"), sem("merged")

        def kn(w, k0, k, c0, n):
            return w.rearrange("(k p) n -> p k n", p=P)[:, k0:k0 + k, c0:c0 + n]

        ffns = [(d["ffn_w_gu"][0, 0], d["ffn_w_down"][0, 0]), (d["ffn_w_gu"][0, 1], d["ffn_w_down"][0, 1]),
                (d["ffn_w_gu"][1, 0], d["ffn_w_down"][1, 0]), (d["ffn_w_gu"][1, 1], d["ffn_w_down"][1, 1]),
                (d["w_gate_up_2"][0], d["w_down_2"][0])]
        MOD_FIRST = [(0, j) for j in range(4)]
        MOD_STEP0 = [[(0, 4), (0, 5)], [(0, 16), (0, 17)], [(1, 10), (1, 11), (1, 17)], [], []]
        MOD_LOOP = [(0, 6, (1, 1)), (1, 0, (1, 1)), (1, 12, (1, 0)), (0, 0, (0, 0)), (0, 0, (0, 0))]
        in_blocks = [0, 512, 1024, 1536, 2048, 2560, 3072, 3592, 4104, 4616, 5128]

        def pieces_of_matrix(w, blocks, kt=KT):
            return [(kn(w, k0, 4, c0, BLK), 4) for c0 in blocks for k0 in range(0, kt, 4)]

        pool_pieces = [(d["pool_w"].rearrange("g (k p) n -> p (g k) n", p=P), 8)]
        qkv_pieces = pieces_of_matrix(d["diff_w_qkv"], range(0, 3 * D, BLK))
        wo_pieces = pieces_of_matrix(d["diff_w_o"], (0, BLK))
        in_pieces = pieces_of_matrix(d["w_in_2"][0], in_blocks)
        pa_pieces = pieces_of_matrix(d["w_proj_a_2"][0], (0, BLK), 4)
        pb_pieces = pieces_of_matrix(d["w_proj_b_2"][0], (0, BLK), 4)
        out_pieces = pieces_of_matrix(d["w_out_2"][0], (0, BLK))

        def slot(buf, n, size):
            s = n.first % size
            return buf[:, s * PIECE:(s + 1) * PIECE]

        TURN = {"piece": 6, A: 2, B: 2, T: 2, "step": 2}

        def per_turn(f):
            n = sum(MOD_LOOP[f][2])
            return {**TURN, M: n, "chunk": n, "acc": 8 * n}

        block = ctx.enter_context(nc.Block())


        class Chain:

            def __init__(self, eng, s):
                self.eng, self.s, self.n = eng, s, 0

            def link(self, ins):
                ins.then_inc(self.s, 1)
                self.n += 1

            def wait(self):
                self.eng.wait_ge(self.s, self.n)

        def broadcast(row, n):
            return row.rearrange("(a n) -> a n", a=1).to_broadcast([P, n])

        @block.sync
        def _(sp):
            n = Tally()

            def free_slot(p):
                if p.i is not None or p.first >= RAW:
                    sp.wait_ge(w_hi, p.back(RAW - 2))
                    sp.wait_ge(w_lo, p.back(RAW - 2))
                s = p.first % RAW
                return raw[:, s * PIECE:(s + 1) * PIECE], raw_landed[s]

            def load_gu(w, j, k0):
                dst, landed = free_slot(n.next("piece"))
                dst = dst.rearrange("p (k g n) -> p k g n", k=4, g=2)
                src = w.rearrange("(k p) (g n) -> p k g n", p=P, g=2)
                for g in range(2):
                    sp.dma_start(dst[:, :, g, :], src[:, k0:k0 + 4, g, bass.ds(j * FFW, FFW)]).then_inc(landed, 16)

            def load_down(w, j):
                dst, landed = free_slot(n.next("piece"))
                dst = dst.rearrange("p (k n) -> p k n", k=2)
                src = w.rearrange("(j k p) n -> p k j n", p=P, k=2)
                for k in range(2):
                    sp.dma_start(dst[:, k, :], src[:, k, bass.ds(j, 1), :].rearrange("p j n -> p (j n)"))\
                      .then_inc(landed, 16)

            def ffn(f):
                gu, down = ffns[f]
                load_gu(gu, 0, 0)
                load_gu(gu, 0, 4)
                with sp.Fori(0, (STEPS - 1) // 2) as i:
                    n.enter(i, {"piece": 6})
                    for e in range(2):
                        load_gu(gu, i * 2 + (e + 1), 0)
                        load_gu(gu, i * 2 + (e + 1), 4)
                        load_down(down, i * 2 + e)
                    n.leave((STEPS - 1) // 2)
                load_down(down, STEPS - 1)

            def matrix(pieces):
                for src, k in pieces:
                    dst, landed = free_slot(n.next("piece"))
                    dst = dst.rearrange("p (k n) -> p k n", k=k)
                    for h in range(2):
                        sp.dma_start(dst[:, h * k // 2:(h + 1) * k // 2, :],
                                     src[:, h * k // 2:(h + 1) * k // 2, :]).then_inc(landed, 16)

            sp.dma_start(prow[0:48, :], d["norm_g"].rearrange("l j (k p) -> (l j k) p", p=P)).then_inc(prm_landed, 16)
            sp.dma_start(prow[48:56, :], d["c"].rearrange("a (k p) -> (a k) p", p=P)).then_inc(prm_landed, 16)
            sp.dma_start(prow[56:64, :], d["norm_mix_g_2"].rearrange("a (k p) -> (a k) p", p=P)).then_inc(prm_landed, 16)
            sp.dma_start(prow[64:72, :], d["norm_ffn_g_2"].rearrange("a (k p) -> (a k) p", p=P)).then_inc(prm_landed, 16)
            sp.dma_start(prow[72:104, :], d["conv_w_2"].rearrange("a j (k p) -> (a j k) p", p=P)).then_inc(prm_landed, 16)
            for l in range(2):
                sp.dma_start(brow[l], d["mod_b"][l, :].rearrange("(k p) -> k p", p=P)).then_inc(prm_landed, 16)
            sp.dma_start(ident[:, :], d["ident"]).then_inc(ident_landed, 16)
            sp.dma_start(x, d["x"][0].rearrange("(t p) n -> p t n", p=P)).then_inc(x_landed, 16)
            ffn(0)
            matrix(pool_pieces)
            ffn(1)
            ffn(2)
            matrix(qkv_pieces)
            matrix(wo_pieces)
            ffn(3)
            matrix(in_pieces)
            matrix(pa_pieces)
            matrix(pb_pieces)
            matrix(out_pieces)
            ffn(4)
            for t in range(TB):
                sp.wait_ge(y_ready, t + 1)
                sp.dma_start(out[0, t * P:(t + 1) * P, :], xnt[:, t, :]).then_inc(out_done, 16)
            sp.wait_ge(out_done, 16 * TB)

        @block.tensor
        def _(pe):
            n = Tally()

            def piece():
                p = n.next("piece")
                pe.wait_ge(w_lo, p.back(-2))
                s = p.first % RING
                return whi[:, s * PIECE:(s + 1) * PIECE], wlo[:, s * PIECE:(s + 1) * PIECE]

            def bank(b):
                f = n.next(b)
                if f.first:
                    pe.wait_ge(drained[b], f.at)
                return ps[:, b, :]

            def three(o, hi, lo, wh, wl, start, stop):
                pe.matmul(o, hi, wh, start=start, stop=False)
                pe.matmul(o, hi, wl, start=False, stop=False)
                return pe.matmul(o, lo, wh, start=False, stop=stop)

            def turned(t, h, first):
                pe.wait_ge(nt_lo, 4 * first + 2 * t + h + 1)

            def columns(kt, first):
                o = [None, None]
                for h in range(kt // 4):
                    wh, wl = piece()
                    wh = wh.rearrange("p (k n) -> p k n", k=4)
                    wl = wl.rearrange("p (k n) -> p k n", k=4)
                    for t in range(TB):
                        if h == 0:
                            o[t] = bank((A, B)[t])
                        if first is not None:
                            turned(t, h, first)
                        for k in range(4):
                            kk = 4 * h + k
                            mm = three(o[t], nth[:, kk, t * P:(t + 1) * P], ntl[:, kk, t * P:(t + 1) * P],
                                       wh[:, k, :], wl[:, k, :], kk == 0, kk == kt - 1)
                        if t == 0 and h == kt // 4 - 1:
                            mm.then_inc(filled[A], 1)
                    mm.then_inc(w_used, 1)

            def sums_free(t, s):
                if s:
                    pe.wait_ge(sums_read[t], s)

            def down(par, start, stop, s=None):
                wh, wl = piece()
                wh = wh.rearrange("p (k h n) -> p k h n", k=2, h=2)
                wl = wl.rearrange("p (k h n) -> p k h n", k=2, h=2)
                for t in range(TB):
                    if start:
                        sums_free(t, s)
                    for h in range(2):
                        for k in range(2):
                            mm = three(ps[:, 2 * t + h, :], hth[:, par, k, t * P:(t + 1) * P],
                                       htl[:, par, k, t * P:(t + 1) * P], wh[:, k, h, :], wl[:, k, h, :],
                                       start and k == 0, stop and k == 1)
                    if stop and t == 0:
                        mm.then_inc(sums_done, 1)
                mm.then_inc(w_used, 1)

            def turn_inner():
                pe.wait_ge(drained[A], n.seen(A))
                pe.wait_ge(drained[B], n.seen(B))
                o = bank(T)
                for k in range(2):
                    for t in range(TB):
                        mm = pe.transpose(o[:, (2 * k + t) * P:(2 * k + t + 1) * P],
                                          sil[:, t, k * P:(k + 1) * P], ident[:, :])
                mm.then_inc(filled[T], 1)

            def sum_chunk():
                c = n.next("chunk")
                pe.wait_ge(acc_step, c.at * KT + KT)
                o = bank(M)
                for q in range(MCH // P):
                    mm = pe.matmul(o[:, q:q + 1], acc[:, q * P:(q + 1) * P], ones[:, 0:1], start=True, stop=True)
                mm.then_inc(filled[M], 1)

            def gate_rows():
                g = n.next("gate")
                pe.wait_ge(diag_ready, g.at + 1)
                for h, b in enumerate((M, T)):
                    pe.matmul(bank(b), ones[:, :], xn[:, h * BLK:(h + 1) * BLK], start=True, stop=True)\
                      .then_inc(filled[b], 1)

            def turn_join():
                j = n.next("join")
                for t in range(TB):
                    pe.wait_ge(xn_ready, j.at * 2 + t + 1)
                    for h in range(2):
                        turn_half(xnt, t, h)

            def turn_half(src, t, h):
                b = ((A, B), (T, M))[t][h]
                o = bank(b)
                for q in range(4):
                    mm = pe.transpose(o[:, q * P:(q + 1) * P], src[:, t, (4 * h + q) * P:(4 * h + q + 1) * P],
                                      ident[:, :])
                mm.then_inc(filled[b], 1)

            def ffn(f, gated):
                first, s = n.next("turned").at, n.next("sums").at
                columns(KT, first)
                turn_inner()
                for _ in MOD_STEP0[f]:
                    sum_chunk()
                def step(par, start):
                    columns(KT, None)
                    pe.wait_ge(drained[T], n.seen(T))
                    down(1 - par, start, False, s)
                    turn_inner()
                step(1, True)
                if MOD_LOOP[f][2][0]:
                    sum_chunk()
                with pe.Fori(0, (STEPS - 3) // 2) as i:
                    n.enter(i, pe_turn(f))
                    for e in range(2):
                        step(e, False)
                        if MOD_LOOP[f][2][1 - e]:
                            sum_chunk()
                    n.leave((STEPS - 3) // 2)
                step(0, False)
                if MOD_LOOP[f][2][1]:
                    sum_chunk()
                if gated:
                    gate_rows()
                    pe.wait_ge(drained[T], n.seen(T) - 1)
                else:
                    pe.wait_ge(drained[T], n.seen(T))
                down(0, False, True)

            def pe_turn(f):
                k = sum(MOD_LOOP[f][2])
                return {"piece": 6, A: 2, B: 2, T: 2, **({M: k, "chunk": k} if k else {})}

            def pool():
                gate_rows()
                wh, wl = piece()
                wh = wh.rearrange("p (k n) -> p k n", k=KT)
                wl = wl.rearrange("p (k n) -> p k n", k=KT)
                s = n.next("sums").at
                for t in range(TB):
                    sums_free(t, s)
                    for g in range(4):
                        pe.wait_ge(pool_lo, g + 1)
                        o = ps[:, 2 * t + g // 2, (g % 2) * 256:(g % 2) * 256 + 256]
                        for k in (2 * g, 2 * g + 1):
                            mm = three(o, nth[:, k, t * P:(t + 1) * P], ntl[:, k, t * P:(t + 1) * P],
                                       wh[:, k, :], wl[:, k, :], k == 2 * g, k == 2 * g + 1)
                    if t == 0:
                        mm.then_inc(sums_done, 1)
                mm.then_inc(w_used, 1)

            def onto_sums(halves, first, k0=0):
                s = n.next("sums").at
                for c in range(2):
                    for h in range(halves):
                        wh, wl = piece()
                        wh = wh.rearrange("p (k n) -> p k n", k=4)
                        wl = wl.rearrange("p (k n) -> p k n", k=4)
                        for t in range(TB):
                            if c == 0 and h == 0:
                                sums_free(t, s)
                            turned(t, (k0 + 4 * h) // 4, first)
                            for k in range(4):
                                kk = k0 + 4 * h + k
                                mm = three(ps[:, 2 * t + c, :], nth[:, kk, t * P:(t + 1) * P],
                                           ntl[:, kk, t * P:(t + 1) * P], wh[:, k, :], wl[:, k, :],
                                           h == 0 and k == 0, h == halves - 1 and k == 3)
                            if c == 1 and h == halves - 1 and t == 0:
                                mm.then_inc(sums_done, 1)
                        mm.then_inc(w_used, 1)

            def diff_attention():
                first = n.next("turned").at
                for _ in range(6):
                    columns(KT, first)
                pe.wait_ge(roped, 2)
                pe.wait_ge(drained[A], n.seen(A))
                pe.wait_ge(drained[B], n.seen(B))

                def scores(h):
                    o = bank(T)
                    for i, c0 in enumerate((0, D)):
                        for t in range(TB):
                            mm = pe.transpose(o[:, (2 * i + t) * P:(2 * i + t + 1) * P],
                                              qkv[:, t, c0 + h * P:c0 + (h + 1) * P], ident[:, :])
                    mm.then_inc(filled[T], 1)
                    pe.wait_ge(drained[T], n.seen(T))
                    for c, b in enumerate((A, B)):
                        o = bank(b)
                        rows = slice(64 * c, 64 * c + 64)
                        for t in range(TB):
                            mm = pe.matmul(o[:, t * S:(t + 1) * S], qkT[rows, h % 2, t * P:(t + 1) * P],
                                           qkT[rows, h % 2, S:2 * S], start=True, stop=True)
                        mm.then_inc(filled[b], 1)

                def mix(h):
                    pe.wait_ge(mix_ready, 2 * h + 2)
                    o = bank(M)
                    for t in range(TB):
                        for k in range(TB):
                            mm = pe.transpose(o[:, (2 * t + k) * P:(2 * t + k + 1) * P],
                                              av[:, t, k * P:(k + 1) * P], ident[:, :])
                    mm.then_inc(filled[M], 1)
                    pe.wait_ge(drained[M], n.seen(M))
                    if h >= 2:
                        pe.wait_ge(out_copied, h - 1)
                    for t in range(TB):
                        for k in range(TB):
                            mm = pe.matmul(ps[:, 2 * (h % 2), t * P:(t + 1) * P], avT[:, t, k, :],
                                           qkv[:, k, 2 * D + h * P:2 * D + (h + 1) * P],
                                           start=(k == 0), stop=(k == 1))
                    mm.then_inc(head_out, 1)

                for h in range(H1 + 1):
                    if h < H1:
                        scores(h)
                    if h:
                        mix(h - 1)
                gate_rows()
                pe.wait_ge(heads_normed, 2)
                for t in range(TB):
                    for h in range(2):
                        turn_half(qkv, t, h)
                onto_sums(2, n.next("turned").at)

            def second_mix():
                first = n.next("turned").at
                pe.wait_ge(mix_landed, 16 * 4)
                o = bank(M)
                for t in range(TB):
                    for k in range(KT):
                        mm = pe.matmul(o[:, 8 * t:8 * t + 8], xnt[:, t, k * P:(k + 1) * P], w8[:, k, :],
                                       start=(k == 0), stop=(k == KT - 1))
                mm.then_inc(filled[M], 1)
                for b in range(3):
                    columns(KT, first)
                for b in range(2):
                    columns(KT, first)
                    pe.wait_ge(conv_in, 2 * b + 2)
                    for t in range(TB):
                        o = bank((T, M)[t])
                        for q in range(4):
                            mm = pe.transpose(o[:, q * P:(q + 1) * P], convin[:, t, q * P:(q + 1) * P], ident[:, :])
                        mm.then_inc(filled[(T, M)[t]], 1)
                for b in range(6):
                    columns(KT, first)

                pe.wait_ge(roped, 4)
                pe.wait_ge(conv_done, 8)
                for r in range(HA // 2):
                    o = bank(T)
                    for i, c0 in enumerate((0, 512)):
                        for t in range(TB):
                            mm = pe.transpose(o[:, (2 * i + t) * P:(2 * i + t + 1) * P],
                                              qkva[:, t, c0 + r * P:c0 + (r + 1) * P], ident[:, :])
                    mm.then_inc(filled[T], 1)
                    pe.wait_ge(drained[T], n.seen(T))
                    for e in range(2):
                        h = 2 * r + e
                        rows = slice(64 * e, 64 * e + 64)
                        o = bank(A)
                        pe.matmul(o[:, 0:P], qkTa[rows, 0:P], qkTa[rows, S:S + P], start=True, stop=True)
                        pe.matmul(o[:, P:3 * P], qkTa[rows, P:S], qkTa[rows, S:2 * S], start=True, stop=True)\
                          .then_inc(filled[A], 1)
                        pe.wait_ge(probs_ready, h + 1)
                        o = bank(M)
                        for q in range(3):
                            mm = pe.transpose(o[:, q * P:(q + 1) * P], pa[:, q * P:(q + 1) * P], ident[:, :])
                        mm.then_inc(filled[M], 1)
                        pe.wait_ge(drained[M], n.seen(M))
                        o = bank(B)
                        v = qkva[:, :, 1024 + h * 64:1024 + (h + 1) * 64]
                        pe.matmul(o[:, 0:64], paT[:, 0:P], v[:, 0, :], start=True, stop=True)
                        pe.matmul(o[:, 64:128], paT[:, P:2 * P], v[:, 0, :], start=True, stop=False)
                        pe.matmul(o[:, 64:128], paT[:, 2 * P:3 * P], v[:, 1, :], start=False, stop=True)\
                          .then_inc(filled[B], 1)

                pe.wait_ge(gated, 1)
                pe.wait_ge(drained[B], n.seen(B))
                o = bank(T)
                for g in range(2):
                    for t in range(TB):
                        mm = pe.transpose(o[0:4, (2 * g + t) * P:(2 * g + t + 1) * P],
                                          small[:, 8 * t + 4 * g:8 * t + 4 * g + 4], ident[:, :])
                mm.then_inc(filled[T], 1)
                pe.wait_ge(rows_done, 1)
                o = bank(M)
                for g, src in enumerate((va_rows[3], va_rows[1])):
                    for t in range(TB):
                        mm = pe.transpose(o[:, (2 * g + t) * 4:(2 * g + t) * 4 + 4], src[:, t * P:(t + 1) * P],
                                          ident[0:4, 0:4])
                mm.then_inc(filled[M], 1)
                pe.wait_ge(late_landed, 32)
                for h in range(HB):
                    o = bank(T)
                    pe.matmul(o[:, 0:S], pick[:, h * P:(h + 1) * P], va_rows[0], start=True, stop=True)\
                      .then_inc(filled[T], 1)
                    o = bank(A)
                    q, k = qkc[:, h, :], qkc[:, 4 + h, :]
                    pe.matmul(o[:, 0:S], k[:, 0:P], q, start=True, stop=True)
                    pe.matmul(o[:, S:S + P], k[:, P:S], q[:, P:S], start=True, stop=True).then_inc(filled[A], 1)
                    pe.wait_ge(drained[A], n.seen(A))
                    o = bank(B)
                    pe.matmul(o[:, 0:129], scT[:, 0:P], vbx[:, 0, h, :], start=True, stop=True)
                    pe.matmul(o[:, 129:258], scT[:, P:S], vbx[:, 0, h, :], start=True, stop=False)
                    pe.matmul(o[:, 129:258], scT[:, S:S + P], vbx[:, 1, h, :], start=False, stop=True)\
                      .then_inc(filled[B], 1)
                pe.wait_ge(y_done, 1)
                for t in range(TB):
                    for h in range(2):
                        turn_half(qkva, t, h)
                first = n.next("turned").at
                onto_sums(1, first, 0)
                for c in range(2):
                    for_b(first)
                pe.wait_ge(merged, 2)
                for t in range(TB):
                    for h in range(2):
                        turn_half(xnt, t, h)
                onto_sums(2, n.next("turned").at)

            def for_b(first):
                wh, wl = piece()
                wh = wh.rearrange("p (k n) -> p k n", k=4)
                wl = wl.rearrange("p (k n) -> p k n", k=4)
                for t in range(TB):
                    o = bank((A, B)[t])
                    turned(t, 1, first)
                    for k in range(4):
                        mm = three(o, nth[:, 4 + k, t * P:(t + 1) * P], ntl[:, 4 + k, t * P:(t + 1) * P],
                                   wh[:, k, :], wl[:, k, :], k == 0, k == 3)
                    if t == 0:
                        mm.then_inc(filled[A], 1)
                mm.then_inc(w_used, 1)

            pe.sem_inc(w_used, 1)
            pe.wait_ge(prm_landed, 16 * 7)
            pe.wait_ge(ident_landed, 16)
            o = bank(A)
            pe.transpose(o[:, 0:NROWS], prow[0:NROWS, :], ident[0:NROWS, 0:NROWS])
            pe.transpose(o[:, 128:200], brow[0][:, :], ident[0:72, 0:72])
            pe.transpose(o[:, 256:328], brow[1][:, :], ident[0:72, 0:72]).then_inc(filled[A], 1)
            pe.wait_ge(consts_set, 3)
            for _ in MOD_FIRST:
                sum_chunk()
            turn_join()
            ffn(0, True)
            turn_join()
            pool()
            turn_join()
            ffn(1, True)
            turn_join()
            ffn(2, True)
            turn_join()
            diff_attention()
            turn_join()
            ffn(3, True)
            turn_join()
            second_mix()
            turn_join()
            ffn(4, False)

        @block.scalar
        def _(act):
            n = Tally()
            own = Chain(act, act_chain)

            def make_hi():
                p = n.next("piece")
                act.wait_ge(raw_landed[p.first % RAW], p.lap(RAW) * 32 + 32)
                if p.i is not None or p.first >= RING:
                    act.wait_ge(w_used, p.back(RING - 2))
                s, r = p.first % RING, p.first % RAW
                nc.scalar.activation(whi[:, s * PIECE:(s + 1) * PIECE], raw[:, r * PIECE:(r + 1) * PIECE],
                                     ACT.Copy).then_inc(w_hi, 1)

            def split(k):
                for _ in range(k):
                    make_hi()

            def full(b):
                f = n.next(b)
                act.wait_ge(filled[b], (n.next("small B") if b == B else f).at + 1)
                return ps[:, b, :]

            def full_with_piece(b, pieces_behind):
                n.next(b)
                act.wait_ge(w_used, n.seen("piece") - (pieces_behind - 1))
                return ps[:, b, :]

            def inner():
                f = n.next(A)
                act.wait_ge(filled[A], f.at + 1)
                nc.scalar.activation(sil[:, 0, :], ps[:, A, 0:FFW], ACT.Silu).then_inc(silu_done, 1)

            def steps(f, k, ahead):
                split(ahead)
                inner()
                full_with_piece(B, k)
                nc.scalar.activation(sil[:, 1, :], ps[:, B, 0:FFW], ACT.Silu).then_inc(silu_done, 1)

            def inner_hi(par):
                o = full(T)
                nc.scalar.activation(hthi[:, par * BLK:(par + 1) * BLK], o, ACT.Copy).then_inc(ht_hi, 1)

            def step(par, k, ahead=3):
                steps(None, k, ahead)
                inner_hi(par)

            def gate_rows(scale):
                g = n.next("gate")
                if g.first:
                    act.wait_ge(gate_used, 2 * g.at)
                for h, b in enumerate((M, T)):
                    o = full(b)
                    nc.scalar.activation(gate[:, h * BLK:(h + 1) * BLK], o, ACT.Copy, scale=scale)\
                      .then_inc(drained[b], 1)

            def squares(t):
                q = n.next("squares")
                act.wait_ge(x_ready, q.at + 1)
                junk = ps[:, (A, T)[t]:(A, T)[t] + 2, :].rearrange("p b n -> p (b n)")
                nc.scalar.activation(junk, x[:, t, :], ACT.Square, accum_out=ss[:, t:t + 1]).then_inc(sq_done, 1)

            def join(split_too=True, squared=1):
                n.next("join")
                for t in range(TB):
                    for _ in range(squared):
                        squares(t)
                    for h in range(2):
                        b = ((A, B), (T, M))[t][h]
                        f = n.next(b)
                        if b == B:
                            n.next("small B")
                        if split_too:
                            act.wait_ge(drained[b], f.at + 1)
                            nc.scalar.activation(nth[:, 4 * h:4 * h + 4, t * P:(t + 1) * P],
                                                 xnt[:, t, h * BLK:(h + 1) * BLK].rearrange("p (k s) -> p k s", k=4),
                                                 ACT.Copy).then_inc(nt_hi, 1)

            def turned_hi():
                for t in range(TB):
                    for h in range(2):
                        o = full(((A, B), (T, M))[t][h])
                        nc.scalar.activation(nth[:, 4 * h:4 * h + 4, t * P:(t + 1) * P],
                                             o.rearrange("p (k s) -> p k s", k=4), ACT.Copy).then_inc(nt_hi, 1)

            def skip_chunks(k):
                for _ in range(k):
                    n.next(M)

            def ffn(f, gated):
                step(0, 3)
                skip_chunks(len(MOD_STEP0[f]))
                pat = MOD_LOOP[f][2]
                turns = (STEPS - 1) // 2 - (f == 4)
                with act.Fori(0, turns) as i:
                    n.enter(i, {"piece": 6, A: 2, B: 2, T: 2, **({M: sum(pat)} if sum(pat) else {})})
                    for e in range(2):
                        step(1 - e, 4)
                        skip_chunks(pat[e])
                    n.leave(turns)
                if f == 4:
                    step(1, 4)
                    step(0, 2, 1)
                if gated:
                    gate_rows(0.5)

            def pool():
                for g in range(4):
                    act.wait_ge(pool_diff, g + 1)
                    src = win[(g + 1) % 2][:, :, 8:8 + S]
                    nc.scalar.activation(nth[:, 2 * g:2 * g + 2, :], src, ACT.Copy).then_inc(pool_hi, 1)
                gate_rows(1.0)
                split(1)

            def diff_attention():
                for b in range(6):
                    split(2)
                    f = n.next(A)
                    act.wait_ge(filled[A], f.at + 1)
                    nc.scalar.activation(qkv[:, 0, b * BLK:(b + 1) * BLK], ps[:, A, :], ACT.Copy)\
                      .then_inc(drained[A], 1)
                    n.next(B)
                act.wait_ge(lam_prod, 1)
                nc.scalar.activation(lam[:, 2:4], lam[:, 0:2], ACT.Exp).then_inc(lam_exp, 1)

                def probs(h):
                    o = full(T)
                    nc.scalar.activation(qkT[:, h % 2, 0:S], o[:, 0:S], ACT.Copy, scale=HD1 ** -0.5)
                    nc.scalar.activation(qkT[:, h % 2, S:2 * S], o[:, S:2 * S], ACT.Copy).then_inc(drained[T], 1)
                    if h:
                        act.wait_ge(mix_ready, 2 * h)
                    for c, b in enumerate((A, B)):
                        act.wait_ge(top_ready, 2 * h + c + 1)
                        o = full(b)
                        for t in range(TB):
                            i = 2 * c + t
                            e = nc.scalar.activation(pr[:, c, t, :], o[:, t * S:(t + 1) * S], ACT.Exp,
                                                     bias=top[:, i:i + 1], accum_out=total[:, i:i + 1])
                            if t:
                                e.then_inc(drained[b], 1)

                def mixed(h):
                    o = full(M)
                    nc.scalar.activation(avT.rearrange("p t k q -> p (t k q)"), o, ACT.Copy).then_inc(drained[M], 1)
                    act.wait_ge(head_out, h + 1)
                    b = 2 * (h % 2)
                    nc.scalar.activation(qkv[:, :, h * P:(h + 1) * P],
                                         ps[:, b, 0:S].rearrange("p (t n) -> p t n", t=TB), ACT.Copy)
                    for t in range(TB):
                        e = nc.scalar.activation(ps[:, b + 1, t * P:(t + 1) * P], ps[:, b, t * P:(t + 1) * P],
                                                 ACT.Square, accum_out=hss[:, 8 * t + h:8 * t + h + 1])
                    e.then_inc(out_copied, 1)

                for h in range(H1 + 1):
                    if h < H1:
                        probs(h)
                    if h:
                        mixed(h - 1)
                gate_rows(1.0)
                turned_hi()
                split(4)

            def second_mix():
                n.next(M)
                for b in range(3):
                    split(2)
                    o = full(A)
                    nc.scalar.activation(qkva[:, 0, b * BLK:(b + 1) * BLK], o, ACT.Copy).then_inc(drained[A], 1)
                    n.next(B)
                for b in range(2):
                    split(2)
                    o = full(A)
                    if b:
                        act.wait_ge(filled[M], n.seen(M))
                    nc.scalar.activation(convin[:, 0, :], o, ACT.Copy).then_inc(conv_in, 1)
                    n.next(B)
                    n.next(T)
                    n.next(M)
                    for q in range(4):
                        act.wait_ge(conv_sum, 4 * b + q + 1)
                        nc.scalar.activation(qkc[:, 4 * b + q, :], qkc[:, 4 * b + q, :], ACT.Silu)\
                          .then_inc(conv_out, 1)
                split(2)
                o = full(A)
                nc.scalar.activation(vbx[:, 0, :, 0:P], o.rearrange("p (h n) -> p h n", h=HB), ACT.Copy)\
                  .then_inc(drained[A], 1)
                n.next(B)
                for b in range(5):
                    split(2)
                    for t in range(TB):
                        if t == 0:
                            o = full(A)
                        else:
                            o = full_with_piece(B, 2)
                        dst = obt[:, t, :] if b == 0 else gab2[:, t, :] if b == 4 else gab[:, t, (b - 1) * BLK:b * BLK]
                        nc.scalar.activation(dst, o, ACT.Sigmoid).then_inc(drained[(A, B)[t]], 1)
                split(2)

                for r in range(HA // 2):
                    o = full(T)
                    nc.scalar.activation(qkTa[:, 0:S], o[:, 0:S], ACT.Copy, scale=HDA ** -0.5)
                    nc.scalar.activation(qkTa[:, S:2 * S], o[:, S:2 * S], ACT.Copy).then_inc(drained[T], 1)
                    for e in range(2):
                        h = 2 * r + e
                        n.next(A)
                        act.wait_ge(top_ready, 2 * H1 + h + 1)
                        nc.scalar.activation(pa[:, 0:P], pa[:, 0:P], ACT.Exp, bias=top[:, 0:1],
                                             accum_out=total[:, 0:1])
                        nc.scalar.activation(pa[:, P:3 * P], pa[:, P:3 * P], ACT.Exp, bias=top[:, 1:2],
                                             accum_out=total[:, 1:2]).then_inc(probs_ready, 1)
                        o = full(M)
                        nc.scalar.activation(paT, o[:, 0:3 * P], ACT.Copy).then_inc(drained[M], 1)
                        n.next(B)
                        n.next("small B")

                n.next(T)
                act.wait_ge(filled[T], n.seen(T))
                own.link(nc.scalar.activation(va_rows[0], ps[0:4, T, S:2 * S], ACT.Abs))
                own.wait()
                own.link(nc.scalar.activation(va_rows[0], va_rows[0], ACT.Exp, scale=-1.0))
                own.wait()
                nc.scalar.activation(va_rows[0], va_rows[0], ACT.Ln, bias=1.0).then_inc(rows_act, 1)
                act.wait_ge(rows_step, 1)
                nc.scalar.activation(va_rows[1], va_rows[1], ACT.Exp, scale=-1.0).then_inc(rows_done, 1)
                n.next(M)
                for h in range(HB):
                    n.next(T)
                    n.next(A)
                    act.wait_ge(decay_in, h + 1)
                    nc.scalar.activation(decay, decay, ACT.Exp, scale=-1.0).then_inc(decay_out, 1)
                    o = full(B)
                    if h:
                        act.wait_ge(den_ready, 2 * h)
                    nc.scalar.activation(total[:, 0:2], o[:, P:P + 130:129], ACT.Abs).then_inc(den_abs, 1)
                    for t in range(TB):
                        act.wait_ge(den_ready, 2 * h + t + 1)
                        nc.scalar.activation(qkva[:, t, 512 + h * P:512 + (h + 1) * P], o[:, 129 * t:129 * t + P],
                                             ACT.Copy, scale=inv[:, t:t + 1])\
                          .then_inc(hb_ready, 1)
                        act.wait_ge(hb_ready, 2 * h + t + 1)
                        e = nc.scalar.activation(junkh, qkva[:, t, 512 + h * P:512 + (h + 1) * P], ACT.Square,
                                                 accum_out=hss[:, 4 * t + h:4 * t + h + 1])
                    e.then_inc(drained[B], 1)
                turned_hi()
                for c in range(2):
                    n.next(A)
                    n.next(B)
                    split(1)
                turned_hi()
                split(4)

            act.sem_inc(w_hi, 1)
            act.wait_ge(cols_copied, 3)
            nc.scalar.activation(cact[:, :], cols[:, C_C:C_C + KT], ACT.Silu).then_inc(cact_ready, 1)
            n.next(A)
            skip_chunks(len(MOD_FIRST))
            split(2)
            join()
            ffn(0, True)
            join(False)
            pool()
            join()
            ffn(1, True)
            join()
            ffn(2, True)
            join()
            diff_attention()
            join()
            ffn(3, True)
            join(squared=2)
            second_mix()
            join()
            ffn(4, False)
            for t in range(TB):
                squares(t)

        @block.vector
        def _(dve):
            n = Tally()
            own = Chain(dve, dve_chain)
            v = nc.vector

            def make_lo():
                p = n.next("piece")
                dve.wait_ge(w_hi, p.back(-2))
                s, r = p.first % RING, p.first % RAW
                hi = whi[:, s * PIECE:(s + 1) * PIECE].bitcast(F32)
                v.tensor_tensor(wlo[:, s * PIECE:(s + 1) * PIECE], raw[:, r * PIECE:(r + 1) * PIECE], hi,
                                ALU.subtract).then_inc(w_lo, 1)

            def split(k):
                for _ in range(k):
                    make_lo()

            def full(b):
                f = n.next(b)
                dve.wait_ge(filled[b], (n.next("small B") if b == B else f).at + 1)
                return ps[:, b, :]

            def full_with_piece(b, pieces_behind):
                n.next(b)
                dve.wait_ge(w_used, n.seen("piece") - (pieces_behind - 1))
                return ps[:, b, :]

            def add_chunk():
                c = n.next("chunk")
                for k in range(KT):
                    if k % 4 == 0:
                        dve.wait_ge(mod_landed[k // 4], c.at * 16 + 16)
                    src = mraw[k // 4][:, k % 4, :]
                    if k == 0:
                        e = v.tensor_scalar(acc, src, cact[:, 0:1], None, ALU.mult)
                    else:
                        dve.wait_ge(acc_step, c.at * KT + k)
                        e = v.scalar_tensor_tensor(acc, src, cact[:, k:k + 1], acc, ALU.mult, ALU.add)
                    e.then_inc(acc_step, 1)

            def keep_chunk(at):
                o = full(M)
                v.tensor_tensor(modc[:, bass.ds(at, 4)], o[:, 0:4], modb[:, bass.ds(at, 4)], ALU.add)\
                 .then_inc(drained[M], 1)

            def chunk_at(layer, chunk):
                return layer * NMOD * KT + chunk * 4

            def inner(k, ahead=3):
                for t, b in enumerate((A, B)):
                    if t == 0:
                        f = n.next(A)
                        s = n.next("silu")
                    else:
                        full_with_piece(B, k)
                        s = n.next("silu")
                    dve.wait_ge(silu_done, s.at + 1)
                    v.tensor_tensor(sil[:, t, :], sil[:, t, :], ps[:, b, FFW:2 * FFW], ALU.mult)\
                     .then_inc(drained[b], 1)

            def inner_lo(par):
                f = n.next(T)
                dve.wait_ge(ht_hi, n.next("inner").at + 1)
                at = slice(par * BLK, (par + 1) * BLK)
                v.tensor_tensor(htlo[:, at], ps[:, T, :], hthi[:, at].bitcast(F32), ALU.subtract)\
                 .then_inc(drained[T], 1)

            def ffn(f, gated):
                split(3)
                inner(3)
                inner_lo(0)
                for l, c in MOD_STEP0[f]:
                    add_chunk()
                    keep_chunk(chunk_at(l, c))
                layer, first, pat = MOD_LOOP[f]
                per = sum(pat)
                turns = (STEPS - 1) // 2 - (f == 4)
                with dve.Fori(0, turns) as i:
                    n.enter(i, {"piece": 6, A: 2, B: 2, T: 2, "silu": 4, "inner": 2,
                                **({M: per, "chunk": per} if per else {})})
                    k = 0
                    for e in range(2):
                        split(3)
                        if pat[e]:
                            add_chunk()
                        inner(4)
                        inner_lo(1 - e)
                        if pat[e]:
                            keep_chunk(i * (4 * per) + (chunk_at(layer, first) + 4 * k))
                            k += 1
                    n.leave(turns)
                if f == 4:
                    split(3)
                    inner(4)
                    inner_lo(1)
                    split(1)
                    inner(2)
                    inner_lo(0)
                if gated:
                    n.next(M)
                    n.next(T)

            def joined(t, gated, by_piece):
                s = n.next("sums 0") if t == 0 else n.next("sums 1")
                if t == 0:
                    dve.wait_ge(sums_done, s.at + 1)
                else:
                    dve.wait_ge(w_used, n.seen("piece") - (by_piece - 1))
                o = ps[:, 2 * t:2 * t + 2, :].rearrange("p b n -> p (b n)")
                if gated:
                    if t == 0:
                        dve.wait_ge(drained[M], n.seen(M))
                        dve.wait_ge(drained[T], n.seen(T))
                    v.tensor_tensor(xnt[:, t, :], o, gate[:, :], ALU.mult).then_inc(sums_read[t], 1)
                    dve.wait_ge(sums_read[t], s.at + 1)
                    v.engine_nop().then_inc(gate_used, 1)
                    own.link(v.tensor_tensor(x[:, t, :], x[:, t, :], xnt[:, t, :], ALU.add))
                else:
                    v.tensor_tensor(x[:, t, :], x[:, t, :], o, ALU.add).then_inc(sums_read[t], 1)
                    dve.wait_ge(sums_read[t], s.at + 1)

            def join(g_cols, shift=None, scale=None, sums=True, gated=True, by_piece=2, split_too=True,
                     final=False):
                if scale is not None:
                    own.link(v.scalar_tensor_tensor(scol[:, :], scale, 1.0, g_cols, ALU.add, ALU.mult))
                    own.wait()
                    g_cols = scol[:, :]
                for t in range(TB):
                    if sums:
                        joined(t, gated, by_piece)
                        if gated:
                            own.wait()
                    elif t == 0:
                        dve.wait_ge(x_landed, 16)
                    nx = n.next("x")
                    v.engine_nop().then_inc(x_ready, 1)
                    if final:
                        r, nx = n.next("rstd"), n.next("x")
                        if t == 0:
                            dve.wait_ge(row_landed, 32)
                        dve.wait_ge(rstd_done, r.at + 1)
                        v.scalar_tensor_tensor(x[:, t, :], x[:, t, :], rstd[:, t:t + 1], row, ALU.mult, ALU.mult)\
                         .then_inc(x_ready, 1)
                        dve.wait_ge(x_ready, nx.at + 1)
                    r = n.next("rstd")
                    dve.wait_ge(rstd_done, r.at + 1)
                    v.tensor_scalar(xnt[:, t, :], x[:, t, :], rstd[:, t:t + 1], None, ALU.mult).then_inc(xn_ready, 1)
                    for h in range(2):
                        b = ((A, B), (T, M))[t][h]
                        o = full(b)
                        for q in range(4):
                            k = 4 * h + q
                            e = v.tensor_scalar(xnt[:, t, k * P:(k + 1) * P], o[:, q * P:(q + 1) * P],
                                                g_cols[:, k:k + 1], None if shift is None else shift[:, k:k + 1],
                                                ALU.mult, *(() if shift is None else (ALU.add,)))
                        e.then_inc(drained[b], 1)
                    if split_too:
                        for h in range(2):
                            dve.wait_ge(nt_hi, n.next("turned half").at + 1)
                            at = nth[:, 4 * h:4 * h + 4, t * P:(t + 1) * P]
                            v.tensor_tensor(ntl[:, 4 * h:4 * h + 4, t * P:(t + 1) * P],
                                            xnt[:, t, h * BLK:(h + 1) * BLK].rearrange("p (k s) -> p k s", k=4),
                                            at.bitcast(F32), ALU.subtract).then_inc(nt_lo, 1)

            def turned_lo():
                for t in range(TB):
                    for h in range(2):
                        b = ((A, B), (T, M))[t][h]
                        n.next(b)
                        if b == B:
                            n.next("small B")
                        dve.wait_ge(nt_hi, n.next("turned half").at + 1)
                        v.tensor_tensor(ntl[:, 4 * h:4 * h + 4, t * P:(t + 1) * P],
                                        ps[:, b, :].rearrange("p (k s) -> p k s", k=4),
                                        nth[:, 4 * h:4 * h + 4, t * P:(t + 1) * P].bitcast(F32), ALU.subtract)\
                         .then_inc(nt_lo, 1)
                        v.engine_nop().then_inc(drained[b], 1)

            def pool():
                v.memset(padded[:, :, 0:8], 0.0)
                own.link(v.memset(padded[:, :, 8 + S:16 + S], 0.0))
                hf = xnt.rearrange("p t (k s) -> p t k s", k=KT)
                for g, w in enumerate(WINDOWS):
                    own.wait()
                    for t in range(TB):
                        e = v.tensor_copy(padded[:, :, 8 + t * P:8 + (t + 1) * P], hf[:, t, 2 * g:2 * g + 2, :])
                    own.link(e)
                    own.wait()
                    src, lo, hi = padded, 1, S + 16
                    own.link(v.tensor_tensor(win[0][:, :, 1:hi], src[:, :, 0:hi - 1], src[:, :, 1:hi], ALU.add))
                    for j in range(1, g + 1):
                        m = 1 << (j - 1)
                        src, dst = win[(j - 1) % 2], win[j % 2]
                        lo, hi = lo + m, hi - m
                        own.wait()
                        own.link(v.tensor_tensor(dst[:, :, lo:hi], src[:, :, lo - m:hi - m], src[:, :, lo + m:hi + m],
                                                 ALU.add))
                    own.wait()
                    if g == 0:
                        dve.wait_ge(edge_landed, 16)
                    o = win[g % 2]
                    for side, at in ((0, 8), (1, S)):
                        e = v.tensor_tensor(o[:, :, at:at + 8], o[:, :, at:at + 8],
                                            edge[:, g, side, :].unsqueeze(1).to_broadcast([P, 2, 8]), ALU.mult)
                    own.link(e)
                    own.wait()
                    diff = win[(g + 1) % 2][:, :, 8:8 + S]
                    v.scalar_tensor_tensor(diff, o[:, :, 8:8 + S], 1.0 / w, padded[:, :, 8:8 + S],
                                           ALU.mult, ALU.subtract).then_inc(pool_diff, 1)
                    dve.wait_ge(pool_hi, g + 1)
                    own.link(v.tensor_tensor(ntl[:, 2 * g:2 * g + 2, :], diff, nth[:, 2 * g:2 * g + 2, :].bitcast(F32),
                                             ALU.subtract))
                    v.engine_nop().then_inc(pool_lo, 1)
                split(1)
                n.next(M)
                n.next(T)
                dve.wait_ge(drained[M], n.seen(M))
                dve.wait_ge(drained[T], n.seen(T))
                dve.wait_ge(row_landed, 16)
                own.link(v.tensor_tensor(gate[:, :], gate[:, :], row, ALU.mult))
                own.wait()

            def diff_attention():
                for b in range(6):
                    split(2)
                    n.next(A)
                    o = full_with_piece(B, 2)
                    v.tensor_copy(qkv[:, 1, b * BLK:(b + 1) * BLK], o).then_inc(drained[B], 1)
                dve.wait_ge(attn_landed, 16 * 3)
                l4 = lamrow.rearrange("p (a b j) -> p a b j", a=2, b=2)
                own.link(v.tensor_tensor(lamt.rearrange("p (a j) -> p a j", a=2), l4[:, :, 0, :], l4[:, :, 1, :],
                                         ALU.mult))
                own.wait()
                v.tensor_reduce(lam[:, 0:2], lamt.rearrange("p (a j) -> p a j", a=2), AX.X, ALU.add)\
                 .then_inc(lam_prod, 1)
                dve.wait_ge(lam_exp, 1)
                own.link(v.tensor_tensor(lam[:, 4:5], lam[:, 3:4], lam[:, 2:3], ALU.subtract))
                own.wait()
                own.link(v.tensor_scalar(lam[:, 5:6], lam[:, 4:5], LAM_INIT, None, ALU.subtract))
                own.wait()

                for h in range(H1):
                    for c, b in enumerate((A, B)):
                        o = full(b)
                        if h:
                            dve.wait_ge(drained[B], n.seen(B) - (b == B))
                        v.tensor_reduce(top[:, 2 * c:2 * c + 2], o.rearrange("p (t k) -> p t k", t=TB), AX.X,
                                        ALU.max, negate=True).then_inc(top_ready, 1)
                    dve.wait_ge(drained[A], n.seen(A))
                    dve.wait_ge(drained[B], n.seen(B))
                    own.link(v.reciprocal(inv, total))
                    own.wait()
                    own.link(v.tensor_scalar(invl[:, 0:2], inv[:, 2:4], lam[:, 5:6], None, ALU.mult))
                    own.wait()
                    if h:
                        dve.wait_ge(filled[M], n.seen(M))
                    for t in range(TB):
                        own.link(v.tensor_scalar(av[:, t, :], pr[:, 0, t, :], inv[:, t:t + 1], None, ALU.mult))
                    own.wait()
                    for t in range(TB):
                        v.scalar_tensor_tensor(av[:, t, :], pr[:, 1, t, :], invl[:, t:t + 1], av[:, t, :],
                                               ALU.mult, ALU.add).then_inc(mix_ready, 1)
                    n.next(T)
                    n.next(M)
                dve.wait_ge(heads_rstd, 1)
                for t in range(TB):
                    o = qkv[:, t, 0:D].rearrange("p (h n) -> p h n", h=H1)
                    own.link(v.tensor_tensor(o, o, hss[:, 8 * t:8 * t + 8].unsqueeze(2).to_broadcast([P, H1, P]),
                                             ALU.mult))
                own.wait()
                for t in range(TB):
                    o = qkv[:, t, 0:D].rearrange("p (h n) -> p h n", h=H1)
                    v.scalar_tensor_tensor(o, o, 1.0 - LAM_INIT, subln.unsqueeze(1).to_broadcast([P, H1, P]),
                                           ALU.mult, ALU.mult).then_inc(heads_normed, 1)
                n.next(M)
                n.next(T)
                turned_lo()
                split(4)

            def second_mix():
                o = full(M)
                dve.wait_ge(mix_landed, 16 * 4)
                v.tensor_tensor(gz, o[:, 0:16].rearrange("p (t g) -> p t g", t=TB),
                                gbias.unsqueeze(1).to_broadcast([P, TB, 8]), ALU.add).then_inc(gated, 1)
                v.engine_nop().then_inc(drained[M], 1)
                v.memset(convT[:, :, 0:3], 0.0)
                own.link(v.memset(vbx[:, :, :, P:P + 1], 1.0))
                for b in range(3):
                    split(2)
                    n.next(A)
                    o = full_with_piece(B, 2)
                    v.tensor_copy(qkva[:, 1, b * BLK:(b + 1) * BLK], o).then_inc(drained[B], 1)
                for b in range(2):
                    split(2)
                    n.next(A)
                    o = full_with_piece(B, 2)
                    if b:
                        dve.wait_ge(filled[M], n.seen(M))
                    v.tensor_copy(convin[:, 1, :], o).then_inc(drained[B], 1)
                    v.engine_nop().then_inc(conv_in, 1)
                    dve.wait_ge(conv_in, 2 * b + 2)
                    v.engine_nop().then_inc(drained[A], 1)
                    dve.wait_ge(roped, 4)
                    o = [full(T), full(M)]
                    for q in range(4):
                        k = 4 * b + q
                        pad = convT[:, q % 2, :]
                        own.wait()
                        for t in range(TB):
                            e = v.tensor_copy(pad[:, 3 + t * P:3 + (t + 1) * P], o[t][:, q * P:(q + 1) * P])
                        own.link(e)
                        own.wait()
                        for j in range(4):
                            tap = cols[:, C_CONV + 8 * j + k:C_CONV + 8 * j + k + 1]
                            src = pad[:, j:j + S]
                            if j == 0:
                                own.link(v.tensor_scalar(qkc[:, k, :], src, tap, None, ALU.mult))
                                own.wait()
                            elif j < 3:
                                own.link(v.scalar_tensor_tensor(qkc[:, k, :], src, tap, qkc[:, k, :],
                                                                ALU.mult, ALU.add))
                                own.wait()
                            else:
                                v.scalar_tensor_tensor(qkc[:, k, :], src, tap, qkc[:, k, :], ALU.mult, ALU.add)\
                                 .then_inc(conv_sum, 1)
                        v.engine_nop().then_inc(conv_done, 1)
                    v.engine_nop().then_inc(drained[T], 1)
                    v.engine_nop().then_inc(drained[M], 1)
                split(2)
                n.next(A)
                o = full_with_piece(B, 2)
                v.tensor_copy(vbx[:, 1, :, 0:P], o.rearrange("p (h n) -> p h n", h=HB)).then_inc(drained[B], 1)
                for b in range(5):
                    split(2)
                    n.next(A)
                    n.next(B)
                    if b == 1:
                        dve.wait_ge(late_landed, 16)
                        dve.wait_ge(drained[A], n.seen(A) - 1)
                        dve.wait_ge(drained[B], n.seen(B) - 1)
                        own.link(v.tensor_tensor(obt, obt, convin[:, 0:1, :].to_broadcast([P, TB, 512]), ALU.mult))
                split(2)
                own.wait()

                dve.wait_ge(mask_landed, 32)
                for r in range(HA // 2):
                    n.next(T)
                    for e in range(2):
                        h = 2 * r + e
                        o = full(A)
                        if h:
                            dve.wait_ge(probs_ready, h)
                        seg = pa.rearrange("p (a k) -> p a k", a=3)
                        osg = o[:, 0:3 * P].rearrange("p (a k) -> p a k", a=3)
                        if h:
                            dve.wait_ge(filled[M], n.seen(M))
                        own.link(v.tensor_tensor(seg[:, 0:3:2, :], osg[:, 0:3:2, :],
                                                 mask_q.unsqueeze(1).to_broadcast([P, 2, P]), ALU.add))
                        own.link(v.tensor_copy(seg[:, 1, :], osg[:, 1, :]))
                        own.wait()
                        v.engine_nop().then_inc(drained[A], 1)
                        own.link(v.tensor_reduce(top[:, 0:1], pa[:, 0:P], AX.X, ALU.max, negate=True))
                        v.tensor_reduce(top[:, 1:2], pa[:, P:3 * P], AX.X, ALU.max, negate=True)\
                         .then_inc(top_ready, 1)
                        dve.wait_ge(probs_ready, h + 1)
                        own.link(v.reciprocal(inv[:, 0:2], total[:, 0:2]))
                        own.wait()
                        n.next(M)
                        o = full(B)
                        for t in range(TB):
                            e2 = v.tensor_scalar(qkva[:, t, h * 64:(h + 1) * 64], o[:, t * 64:(t + 1) * 64],
                                                 inv[:, t:t + 1], None, ALU.mult)
                        e2.then_inc(drained[B], 1)

                v.engine_nop().then_inc(attention_over, 1)
                r0, r1, r2, r3 = va_rows
                o = full(T)
                i_row, f_row = o[0:4, 0:S], o[0:4, S:2 * S]
                dve.wait_ge(rows_act, 1)
                own.link(v.tensor_scalar(r1, f_row, 0.0, None, ALU.min))
                own.wait()
                own.link(v.tensor_tensor(r1, r1, r0, ALU.subtract))
                own.wait()
                own.link(v.tensor_tensor_scan(r2, ones[0:4, 0:1].to_broadcast([4, S]), r1, 0.0, ALU.mult, ALU.add))
                own.wait()
                own.link(v.tensor_tensor(r3, i_row, r2, ALU.subtract))
                own.wait()
                v.engine_nop().then_inc(drained[T], 1)
                own.link(v.tensor_tensor_scan(r0, r3, r3, 0.0, ALU.max, ALU.max))
                own.wait()
                own.link(v.tensor_tensor(r1, r2, r0, ALU.add))
                v.engine_nop().then_inc(rows_step, 1)
                o = full(M)
                v.tensor_copy(agate.rearrange("p g t h -> p (g t h)"), o[:, 0:16]).then_inc(drained[M], 1)
                dve.wait_ge(drained[M], n.seen(M))
                for h in range(HB):
                    o = full(T)
                    if h:
                        own.wait()
                    for s, (m0, d0) in enumerate(((0, 0), (P, S))):
                        a = agate[:, 0, s, h:h + 1]
                        own.link(v.scalar_tensor_tensor(decay[:, d0:d0 + P], o[:, m0:m0 + P], a, mask_k,
                                                        ALU.subtract, ALU.max))
                    own.link(v.tensor_scalar(decay[:, P:S], o[:, P:S], agate[:, 0, 0, h:h + 1], 0.0,
                                             ALU.subtract, ALU.max))
                    v.engine_nop().then_inc(drained[T], 1)
                    v.engine_nop().then_inc(decay_in, 1)
                    o = full(A)
                    dve.wait_ge(decay_out, h + 1)
                    if h:
                        dve.wait_ge(filled[B], n.seen("small B"))
                    own.link(v.scalar_tensor_tensor(scT, o[:, 0:3 * P], HDB ** -0.5, decay, ALU.mult, ALU.mult))
                    v.engine_nop().then_inc(drained[A], 1)
                    o = full(B)
                    if h:
                        dve.wait_ge(hb_ready, 2 * h)
                    dve.wait_ge(den_abs, h + 1)
                    own.link(v.tensor_tensor(total[:, 0:2], total[:, 0:2], agate[:, 1, :, h], ALU.max))
                    own.wait()
                    for t in range(TB):
                        v.reciprocal(inv[:, t:t + 1], total[:, t:t + 1]).then_inc(den_ready, 1)
                dve.wait_ge(heads_rstd, 2)
                for t in range(TB):
                    o = qkva[:, t, 512:D].rearrange("p (h n) -> p h n", h=HB)
                    own.link(v.tensor_tensor(o, o, hss[:, 4 * t:4 * t + 4].unsqueeze(2).to_broadcast([P, HB, P]),
                                             ALU.mult))
                own.wait()
                own.link(v.tensor_tensor(qkva[:, :, 512:D], qkva[:, :, 512:D], obt, ALU.mult))
                v.engine_nop().then_inc(y_done, 1)
                turned_lo()

                for t in range(TB):
                    s = n.next("sums 0") if t == 0 else n.next("sums 1")
                    if t == 0:
                        dve.wait_ge(sums_done, s.at + 1)
                    else:
                        dve.wait_ge(w_used, n.seen("piece") - 1)
                    for c in range(2):
                        own.link(v.tensor_tensor(xnt[:, t, c * BLK:(c + 1) * BLK], ps[:, 2 * t + c, :],
                                                 gab[:, t, c * BLK:(c + 1) * BLK], ALU.mult))
                    v.engine_nop().then_inc(sums_read[t], 1)
                for c in range(2):
                    split(1)
                    sig = gab[:, :, 2 * BLK:3 * BLK] if c == 0 else gab2
                    for t, b in enumerate((A, B)):
                        if t == 0:
                            o = full(A)
                        else:
                            o = full_with_piece(B, 2)
                        own.link(v.tensor_tensor(sig[:, t, :], o, sig[:, t, :], ALU.mult))
                        v.engine_nop().then_inc(drained[b], 1)
                    own.wait()
                    for t in range(TB):
                        own.link(v.tensor_tensor(xnt[:, t, c * BLK:(c + 1) * BLK], xnt[:, t, c * BLK:(c + 1) * BLK],
                                                 sig[:, t, :], ALU.add))
                own.wait()
                for t in range(TB):
                    v.engine_nop().then_inc(merged, 1)
                turned_lo()
                split(4)

            v.engine_nop().then_inc(w_lo, 1)
            o = full(A)
            v.tensor_copy(cols[:, :], o[:, 0:NROWS]).then_inc(cols_copied, 1)
            v.tensor_copy(modb[:, 0:72], o[:, 128:200]).then_inc(cols_copied, 1)
            v.tensor_copy(modb[:, 72:144], o[:, 256:328]).then_inc(cols_copied, 1)
            v.engine_nop().then_inc(drained[A], 1)
            dve.wait_ge(cact_ready, 1)
            for l, c in MOD_FIRST:
                add_chunk()
                keep_chunk(chunk_at(l, c))
            split(2)

            def modulated(layer, j):
                return norm_col(layer, j), mod_cols(layer, 3 * j), mod_cols(layer, 3 * j + 1)

            dve.wait_ge(drained[M], n.seen(M))
            join(*modulated(0, 0), sums=False)
            ffn(0, True)
            join(*modulated(0, 1), split_too=False)
            pool()
            join(*modulated(0, 2))
            ffn(1, True)
            join(*modulated(1, 0))
            ffn(2, True)
            join(*modulated(1, 1))
            diff_attention()
            join(*modulated(1, 2))
            ffn(3, True)
            join(cols[:, C_MIX:C_MIX + KT], final=True)
            second_mix()
            join(cols[:, C_FFN:C_FFN + KT], gated=False)
            ffn(4, False)
            for t in range(TB):
                joined(t, False, 0)
                n.next("x")
                v.engine_nop().then_inc(x_ready, 1)
                r = n.next("rstd")
                if t == 0:
                    dve.wait_ge(row_landed, 48)
                dve.wait_ge(rstd_done, r.at + 1)
                v.scalar_tensor_tensor(xnt[:, t, :], x[:, t, :], rstd[:, t:t + 1], row, ALU.mult, ALU.mult)\
                 .then_inc(y_ready, 1)

        @block.gpsimd
        def _(pool):
            n = Tally()
            own = Chain(pool, pool_chain)
            g = nc.gpsimd

            def load_chunk(layer, chunk):
                c = n.next("chunk")
                src = d["mod_w"][layer].rearrange("(k p) n -> p k n", p=P)
                for h in range(2):
                    if c.first:
                        pool.wait_ge(acc_step, c.at * KT + (4 * h + 4 - KT))
                    pool.dma_start(mraw[h], src[:, 4 * h:4 * h + 4, bass.ds(chunk * MCH, MCH)])\
                        .then_inc(mod_landed[h], 16)

            def load_chunks(f):
                for l, c in MOD_STEP0[f]:
                    load_chunk(l, c)
                layer, first, pat = MOD_LOOP[f]
                per = sum(pat)
                if per:
                    with pool.Fori(0, (STEPS - 1) // 2) as i:
                        n.enter(i, {"chunk": per})
                        for k in range(per):
                            load_chunk(layer, i * per + (first + k))
                        n.leave((STEPS - 1) // 2)

            def diagonals(layer, v):
                cols_ = mod_cols(layer, v)
                g.tensor_tensor(diag, ident[:, :].unsqueeze(1).to_broadcast([P, KT, P]),
                                cols_.unsqueeze(2).to_broadcast([P, KT, P]), ALU.mult).then_inc(diag_ready, 1)

            def rms(times=1):
                for t in range(TB):
                    for _ in range(times):
                        r = n.next("rstd").at
                        pool.wait_ge(sq_done, r + 1)
                        g.tensor_scalar(ss[:, t:t + 1], ss[:, t:t + 1], 1.0 / D, EPS, ALU.mult, ALU.add)\
                         .then_inc(rstd_v, 1)
                        pool.wait_ge(rstd_v, r + 1)
                        g.tensor_tensor(rstd[:, t:t + 1], ss[:, t:t + 1], power[:, 0:1], ALU.pow)\
                         .then_inc(rstd_done, 1)

            def pool_signal(s):
                g.engine_nop().then_inc(s, 1)

            def head_rms(k, width):
                own.link(g.tensor_scalar(hss[:, 0:k], hss[:, 0:k], 1.0 / width, EPS, ALU.mult, ALU.add))
                own.wait()
                g.tensor_tensor(hss[:, 0:k], hss[:, 0:k], power[:, 0:1].to_broadcast([P, k]), ALU.pow)\
                 .then_inc(heads_rstd, 1)

            def rope(x1, x2, cos, sin, tmp):
                own.wait()
                g.tensor_tensor(tmp[0], x1, cos, ALU.mult)
                g.tensor_tensor(tmp[1], x2, sin, ALU.mult)
                g.tensor_tensor(tmp[2], x2, cos, ALU.mult)
                own.link(g.tensor_tensor(tmp[3], x1, sin, ALU.mult))
                own.wait()
                g.tensor_tensor(x1, tmp[0], tmp[1], ALU.subtract)
                own.link(g.tensor_tensor(x2, tmp[2], tmp[3], ALU.add))

            def skip(k=1, **kw):
                for name, b in (("a", A), ("b", B), ("t", T), ("m", M)):
                    n.n[b] = n.n.get(b, 0) + kw.get(name, 0) * k

            def ffn(f):
                load_chunks(f)
                skip(a=STEPS, b=STEPS, t=STEPS, m=len(MOD_STEP0[f]) + (STEPS - 1) // 2 * sum(MOD_LOOP[f][2]))

            def join(times=1):
                rms(times)
                skip(a=1, b=1, t=1, m=1)

            def diag_of(layer, v):
                pool.wait_ge(drained[M], n.seen(M))
                diagonals(layer, v)
                skip(t=1, m=1)

            g.memset(power[:, :], -0.5).then_inc(consts_set, 1)
            g.memset(ones[:, :], 1.0).then_inc(consts_set, 1)
            g.memset(small[:, :], 0.0).then_inc(consts_set, 1)
            pool.wait_ge(consts_set, 3)
            for l, c in MOD_FIRST:
                load_chunk(l, c)
            skip(a=1, m=len(MOD_FIRST))
            pool.dma_start(row, broadcast(d["pool_scale"], D)).then_inc(row_landed, 16)
            pool.dma_start(edge.rearrange("p g e j -> p (g e j)"), d["edge"]).then_inc(edge_landed, 16)
            join()
            ffn(0)
            pool.wait_ge(nt_lo, 4)
            diag_of(0, 2)
            join()
            pool.wait_ge(pool_lo, 4)
            diag_of(0, 5)
            join()
            ffn(1)
            pool.wait_ge(nt_lo, 8)
            diag_of(0, 8)
            pool.wait_ge(sums_read[0], 2)
            pool.dma_start(subln, broadcast(d["diff_subln_g"], P)).then_inc(attn_landed, 16)
            pool.dma_start(rope1.rearrange("p c t j -> p (c t j)"), d["rope1"]).then_inc(attn_landed, 16)
            pool.dma_start(lamrow, broadcast(d["diff_lambda"].rearrange("a j -> (a j)"), 256)).then_inc(attn_landed, 16)
            join()
            ffn(2)
            pool.wait_ge(nt_lo, 12)
            diag_of(1, 2)
            join()

            skip(a=4, b=4)
            pool.wait_ge(drained[A], n.seen(A))
            pool.wait_ge(drained[B], n.seen(B))
            pool.wait_ge(nt_lo, 16)
            pool.wait_ge(attn_landed, 48)
            for t in range(TB):
                heads = qkv[:, t, 0:2 * D].rearrange("p (h j) -> p h j", j=HD1)
                half = ROT // 2
                c, s = (rope1[:, i, t, :].unsqueeze(1).to_broadcast([P, 4 * H1, half]) for i in range(2))
                tmp = [xn[:, 256 * i:256 * i + 256].rearrange("p (h j) -> p h j", j=half) for i in range(4)]
                rope(heads[:, :, 0:half], heads[:, :, half:ROT], c, s, tmp)
                own.wait()
                pool_signal(roped)
            skip(a=2, b=2)
            skip(H1, a=1, b=1, t=1, m=1)
            diag_of(1, 5)
            pool.wait_ge(out_copied, H1)
            head_rms(2 * H1, P)
            skip(a=1, b=1, t=1, m=1)
            join()
            ffn(3)
            pool.wait_ge(nt_lo, 24)
            diag_of(1, 8)
            pool.wait_ge(drained[M], n.seen(M))
            pool.dma_start(mask_q, d["mask_q"]).then_inc(mask_landed, 16)
            pool.dma_start(mask_k, d["mask_k"]).then_inc(mask_landed, 16)
            pool.dma_start(row, broadcast(d["final_g"], D)).then_inc(row_landed, 16)
            pool.dma_start(w8, d["w_in_2"][0].rearrange("(k p) n -> p k n", p=P)[:, :, GATE_COL:GATE_COL + 8])\
                .then_inc(mix_landed, 16)
            pool.dma_start(gbias[:, 0:4], broadcast(d["b_igate_2"][0], 4)).then_inc(mix_landed, 16)
            pool.dma_start(gbias[:, 4:8], broadcast(d["b_fgate_2"][0], 4)).then_inc(mix_landed, 16)
            pool.dma_start(rope2.rearrange("p c t j -> p (c t j)"), d["rope2"]).then_inc(mix_landed, 16)
            join(2)

            skip(m=1)
            skip(a=2, b=2)
            pool.wait_ge(drained[M], n.seen(M))
            pool.wait_ge(drained[A], n.seen(A))
            pool.wait_ge(drained[B], n.seen(B))
            pool.wait_ge(nt_lo, 28)
            pool.wait_ge(mix_landed, 64)
            for t in range(TB):
                heads = qkva[:, t, 0:1024].rearrange("p (h j) -> p h j", j=HDA)
                half = HDA // 2
                c, s = (rope2[:, i, t, :].unsqueeze(1).to_broadcast([P, 2 * HA, half]) for i in range(2))
                tmp = [xn[:, 512 * i:512 * i + 512].rearrange("p (h j) -> p h j", j=half) for i in range(4)]
                rope(heads[:, :, 0:half], heads[:, :, half:HDA], c, s, tmp)
                own.wait()
                pool_signal(roped)
            pool.wait_ge(conv_done, 8)
            pool.dma_start(convin[:, 0, :], broadcast(d["mlstm_norm_g_2"][0], 512)).then_inc(late_landed, 16)
            skip(a=9, b=9, t=2, m=2)
            skip(HA, a=1, b=1, m=1)
            skip(t=HA // 2)
            pool.wait_ge(attention_over, 1)
            pool.dma_start(pick, d["pick"]).then_inc(late_landed, 16)
            skip(t=1, m=1)
            skip(HB, a=1, b=1, t=1)
            pool.wait_ge(drained[B], n.seen(B))
            head_rms(2 * HB, P)
            join()
            pool.dma_start(row, broadcast(d["norm_final_g_2"], D)).then_inc(row_landed, 16)
            rms()


def kernel(**inputs):
    import concourse.bacc as bacc
    from concourse.bass_utils import run_bass_kernel_spmd

    nc = bacc.Bacc("TRN2", target_bir_lowering=False, num_devices=1)
    arrays = {name: np.ascontiguousarray(inputs[name]) for name in INPUTS}
    arrays.update(constants())
    args = {name: nc.dram_tensor(f"in_{name}", a.shape, mybir.dt.from_np(a.dtype), kind="ExternalInput").ap()
            for name, a in arrays.items()}
    out = nc.dram_tensor("out", (1, S, D), F32, kind="ExternalOutput").ap()
    build(nc, args, out)
    result = run_bass_kernel_spmd(nc, [{f"in_{name}": a for name, a in arrays.items()}], core_ids=[0])
    return result.results[0]["out"]
```

```python
import math
from collections import namedtuple
from contextlib import ExitStack

import numpy as np

import concourse.bass as bass
from concourse import mybir

F32 = mybir.dt.float32
F32R = mybir.dt.float32r
ALU = mybir.AluOpType
ACT = mybir.ActivationFunctionType
AX = mybir.AxisListType

P = 128
D = 1024
S = 256
TB = S // P
KT = D // P
FF = 2816
EPS = 1e-6
PIECE = 2048
BLK = 512
FFW = 256
STEPS = FF // FFW
RAW = 3
RING = 6
NMOD = 9
MCH = 512
A, B, T, M = 4, 5, 6, 7
WINDOWS = (2, 4, 8, 16)
H1, HD1 = 8, 64
ROT = HD1 // 4
HA, HDA = 8, 64
HB, HDB = 4, 128
LAM_INIT = 0.8 - 0.6 * math.exp(-0.3 * 1)
IN_COLS = 5640
GATE_COL = 3584
HUGE = 1e30


class Nth:

    def __init__(self, first, i=None, per=0):
        self.first, self.i, self.per = first, i, per
        self.at = first if i is None else i * per + first

    def back(self, k):
        return self.first - k if self.i is None else self.i * self.per + (self.first - k)

    def lap(self, size):
        n = self.first // size
        return n if self.i is None else self.i * (self.per // size) + n


class Tally:

    def __init__(self):
        self.n, self.i, self.per, self.start = {}, None, {}, {}

    def next(self, name):
        n = self.n.get(name, 0)
        self.n[name] = n + 1
        if self.i is None:
            return Nth(n)
        return Nth(n, self.i, self.per[name])

    def seen(self, name):
        n = self.n.get(name, 0)
        return n if self.i is None else self.i * self.per[name] + n

    def enter(self, i, per):
        self.i, self.per, self.start = i, per, {k: self.n.get(k, 0) for k in per}

    def leave(self, turns):
        for k, per in self.per.items():
            assert self.n.get(k, 0) - self.start[k] == per, (k, per)
            self.n[k] = self.start[k] + per * turns
        self.i = None


def constants():
    f = np.float32
    t = np.arange(S, dtype=f)
    inv1 = (f(1.0) / (f(500000.0) ** (np.arange(0, ROT, 2, dtype=f) / f(ROT)))).astype(f)
    ang1 = (t[:, None] * inv1[None, :]).astype(f)
    half = HDA // 2
    inv2 = (f(10000.0) ** (-np.arange(half, dtype=f) / f(half))).astype(f)
    ang2 = (t[:, None] * inv2[None, :]).astype(f)

    def rows(a):
        return a.reshape(TB, P, -1).transpose(1, 0, 2)

    rope1 = np.stack([rows(np.cos(ang1)), rows(np.sin(ang1))], 1).astype(f)
    rope2 = np.stack([rows(np.cos(ang2)), rows(np.sin(ang2))], 1).astype(f)
    edge = np.ones((4, 2, 8), f)
    for g, w in enumerate(WINDOWS):
        for j in range(8):
            for side, tok in ((0, j), (1, S - 8 + j)):
                n = min(tok + w // 2, S) - max(tok - w // 2, 0)
                edge[g, side, j] = f(w) / f(n)
    q, k = np.arange(P)[:, None], np.arange(P)[None, :]
    mask_q = np.where(k <= q, 0.0, -HUGE).astype(f)
    mask_k = np.where(q <= k, 0.0, HUGE).astype(f)
    pick = np.zeros((4, 4, P), f)
    for h in range(4):
        pick[h, h] = 1.0
    return {
        "ident": np.eye(P, dtype=f),
        "rope1": rope1.reshape(P, -1), "rope2": rope2.reshape(P, -1),
        "edge": np.broadcast_to(edge.reshape(1, -1), (P, 64)).copy(),
        "mask_q": mask_q, "mask_k": mask_k, "pick": pick.reshape(4, 4 * P),
    }


INPUTS = ["x", "c", "mod_w", "mod_b", "norm_g", "ffn_w_gu", "ffn_w_down", "pool_w", "pool_scale",
          "diff_w_qkv", "diff_lambda", "diff_subln_g", "diff_w_o", "final_g", "norm_mix_g_2",
          "w_in_2", "conv_w_2", "b_igate_2", "b_fgate_2", "mlstm_norm_g_2", "w_proj_a_2",
          "w_proj_b_2", "w_out_2", "norm_ffn_g_2", "w_gate_up_2", "w_down_2", "norm_final_g_2"]


def build(nc, d, out):
    ctx = ExitStack()

    def sb(name, cols, dt=F32, parts=P):
        return ctx.enter_context(nc.sbuf_tensor(name, [parts, cols], dt))

    def sem(name):
        return ctx.enter_context(nc.semaphore(name))

    with ctx:
        ps = ctx.enter_context(nc.psum_tensor("ps", [P, 8, BLK], F32))
        raw = sb("raw", RAW * PIECE)
        whi = sb("whi", RING * PIECE, F32R)
        wlo = sb("wlo", RING * PIECE, F32R)
        xres = sb("xres", TB * D)
        nthi = sb("nthi", KT * S, F32R)
        ntlo = sb("ntlo", KT * S, F32R)
        xn = sb("xn", TB * D)
        gate = sb("gate", D)
        hthi = sb("hthi", 2 * 2 * S, F32R)
        htlo = sb("htlo", 2 * 2 * S, F32R)
        arena = sb("arena", 9984)
        ident = sb("ident", P)
        ones = sb("ones", P)
        cols = sb("cols", 104)
        modb = sb("modb", 2 * NMOD * KT)
        modc = sb("modc", 2 * NMOD * KT)
        scol = sb("scol", KT)
        cact = sb("cact", KT)
        ss = sb("ss", 2)
        rstd = sb("rstd", 2)
        rdiag = sb("rdiag", TB * P)
        power = sb("power", 2)
        small = sb("small", 96)

        x = xres[:, :].rearrange("p (t n) -> p t n", t=TB)
        xnt = xn[:, :].rearrange("p (t n) -> p t n", t=TB)
        nth = nthi[:, :].rearrange("p (k s) -> p k s", k=KT)
        ntl = ntlo[:, :].rearrange("p (k s) -> p k s", k=KT)
        hth = hthi[:, :].rearrange("p (b k s) -> p b k s", b=2, k=2)
        htl = htlo[:, :].rearrange("p (b k s) -> p b k s", b=2, k=2)
        C_NORM, C_C, C_MIX, C_FFN, C_CONV = 0, 48, 56, 64, 72
        NROWS = 104

        def norm_col(layer, j):
            at = C_NORM + (3 * layer + j) * KT
            return cols[:, at:at + KT]

        def mod_cols(layer, v):
            at = (layer * NMOD + v) * KT
            return modc[:, at:at + KT]

        class Arena:

            def __init__(self):
                self.at = 0

            def take(self, n, parts=P):
                self.at += n
                assert self.at <= 9984, self.at
                return arena[0:parts, self.at - n:self.at]

        ar = Arena()
        mraw = [ar.take(4 * MCH).rearrange("p (k n) -> p k n", k=4) for _ in range(2)]
        acc = ar.take(MCH)
        mfirst = mraw + [arena[:, 5504 + 4 * MCH * i:5504 + 4 * MCH * (i + 1)].rearrange("p (k n) -> p k n", k=4)
                         for i in range(2)]
        sil = ar.take(TB * FFW).rearrange("p (t n) -> p t n", t=TB)
        prow = ar.take(P)
        brow = [ar.take(P, 72) for _ in range(2)]

        row = arena[:, 9984 - D:9984]
        ar = Arena()
        ar.at = 4 * MCH * 2 + MCH + TB * FFW
        padded = ar.take(2 * (S + 16)).rearrange("p (k s) -> p k s", k=2)
        win = [ar.take(2 * (S + 16)).rearrange("p (k s) -> p k s", k=2) for _ in range(2)]
        edge = ar.take(64).rearrange("p (g e j) -> p g e j", g=4, e=2)
        ar = Arena()
        qkv = ar.take(TB * 3 * D).rearrange("p (t n) -> p t n", t=TB)
        qkT = ar.take(2 * BLK).rearrange("p (b n) -> p b n", b=2)
        pr = ar.take(2 * BLK).rearrange("p (c t k) -> p c t k", c=2, t=2)
        av = ar.take(BLK).rearrange("p (t k) -> p t k", t=2)
        avT = ar.take(BLK).rearrange("p (t k q) -> p t k q", t=2, k=2)
        subln = ar.take(P)
        rope1 = ar.take(32).rearrange("p (c t j) -> p c t j", c=2, t=2)
        lamrow = ar.take(256)
        lamt = ar.take(128)
        ar = Arena()
        qkva = ar.take(TB * 1536).rearrange("p (t n) -> p t n", t=TB)
        vbx = ar.take(TB * 516).rearrange("p (t h n) -> p t h n", t=TB, h=4)
        obt = ar.take(TB * 512).rearrange("p (t n) -> p t n", t=TB)
        gab = ar.take(TB * 1536).rearrange("p (t n) -> p t n", t=TB)
        gab2 = gate[:, :].rearrange("p (t n) -> p t n", t=TB)
        w8 = ar.take(64).rearrange("p (k n) -> p k n", k=KT)
        rope2 = ar.take(128).rearrange("p (c t j) -> p c t j", c=2, t=2)
        rest = ar.at
        convin = ar.take(TB * 512).rearrange("p (t n) -> p t n", t=TB)
        convT = ar.take(2 * 259).rearrange("p (b n) -> p b n", b=2)
        ar.at = rest
        qTa, kTa = rdiag[:, :], ar.take(S)
        pa2 = [ar.take(384) for _ in range(2)]
        paT = ar.take(384)
        ar.at = rest
        decay = ar.take(384)
        scT = ar.take(384)
        pick = ar.take(4 * P, 4)
        junkh = ar.take(P)
        va_rows = [qkva[0:4, t, 1024 + 256 * i:1280 + 256 * i] for t in range(2) for i in range(2)]

        qkc = xn[:, :].rearrange("p (k s) -> p k s", k=KT)
        diag = xn[:, 0:D].rearrange("p (k n) -> p k n", k=KT)
        mask_q, mask_k = modb[:, 0:P], modc[:, 0:P]
        gz = small[:, 0:16].rearrange("p (t g) -> p t g", t=TB)
        gbias = small[:, 16:24]
        agate = small[:, 24:40].rearrange("p (g t h) -> p g t h", g=2, t=TB)
        lam = small[:, 0:8]
        top, total, inv, invl = (small[:, 40 + 4 * i:44 + 4 * i] for i in range(4))
        hss = small[:, 56:72]

        raw_landed = [sem(f"raw_landed{i}") for i in range(RAW)]
        w_hi, w_lo, w_used = sem("w_hi"), sem("w_lo"), sem("w_used")
        filled = {b: sem(f"filled{b}") for b in (A, B, T, M)}
        drained = {b: sem(f"drained{b}") for b in (A, B, T, M)}
        sums_done = sem("sums_done")
        sums_read = [sem("sums_read0"), sem("sums_read1")]
        silu_done = sem("silu_done")
        h_ready = sem("h_ready")
        ht_hi, ht_lo = sem("ht_hi"), sem("ht_lo")
        mod_landed = [sem("mod_landed0"), sem("mod_landed1")]
        first_landed, first_used = [sem(f"first_landed{i}") for i in range(4)], sem("first_used")
        c_landed, g_ready = sem("c_landed"), sem("g_ready")
        acc_step, acc_ready, acc_used, modc_ready = sem("acc_step"), sem("acc_ready"), sem("acc_used"), sem("modc_ready")
        diag_ready, gate_ready, gate_step = sem("diag_ready"), sem("gate_ready"), sem("gate_step")
        gate_used = sem("gate_used")
        x_ready, x_step, sq_done, rstd_v, rstd_done = sem("x_ready"), sem("x_step"), sem("sq_done"), sem("rstd_v"), sem("rstd_done")
        rdiag_ready, hf_ready, nt_hi, nt_lo = sem("rdiag_ready"), sem("hf_ready"), sem("nt_hi"), sem("nt_lo")
        x_landed, prm_landed, ident_landed = sem("x_landed"), sem("prm_landed"), sem("ident_landed")
        cols_copied = sem("cols_copied")
        row_landed, edge_landed, attn_landed, mix_landed, late_landed = (
            sem("row_landed"), sem("edge_landed"), sem("attn_landed"), sem("mix_landed"), sem("late_landed"))
        consts_set, cact_ready = sem("consts_set"), sem("cact_ready")
        out_done, y_ready = sem("out_done"), sem("y_ready")
        dve_chain, pool_chain, act_chain = sem("dve_chain"), sem("pool_chain"), sem("act_chain")
        pool_diff, pool_hi, pool_lo = sem("pool_diff"), sem("pool_hi"), sem("pool_lo")
        lam_prod, lam_exp = sem("lam_prod"), sem("lam_exp")
        roped = sem("roped")
        top_ready, probs_ready, mix_ready, head_out, out_copied = (
            sem("top_ready"), sem("probs_ready"), sem("mix_ready"), sem("head_out"), sem("out_copied"))
        heads_v, heads_rstd, heads_normed = sem("heads_v"), sem("heads_rstd"), sem("heads_normed")
        conv_in, conv_sum, conv_out, conv_done = sem("conv_in"), sem("conv_sum"), sem("conv_out"), sem("conv_done")
        gated, ob_scaled, gab_read, gab_ready = sem("gated"), sem("ob_scaled"), sem("gab_read"), sem("gab_ready")
        mask_landed, attention_over = sem("mask_landed"), sem("attention_over")
        rows_step, rows_act, rows_done = sem("rows_step"), sem("rows_act"), sem("rows_done")
        hb_ready, den_abs = sem("hb_ready"), sem("den_abs")
        den_ready, decay_in, decay_out = sem("den_ready"), sem("decay_in"), sem("decay_out")
        y_done, merged = sem("y_done"), sem("merged")

        def kn(w, k0, k, c0, n):
            return w.rearrange("(k p) n -> p k n", p=P)[:, k0:k0 + k, c0:c0 + n]

        ffns = [(d["ffn_w_gu"][0, 0], d["ffn_w_down"][0, 0]), (d["ffn_w_gu"][0, 1], d["ffn_w_down"][0, 1]),
                (d["ffn_w_gu"][1, 0], d["ffn_w_down"][1, 0]), (d["ffn_w_gu"][1, 1], d["ffn_w_down"][1, 1]),
                (d["w_gate_up_2"][0], d["w_down_2"][0])]
        MOD_FIRST = [(0, j) for j in range(4)]
        MOD_LOOP = [(0, 4, (1, 1), 5), (1, 0, (1, 1), 5), (1, 10, (1, 1), 4), (0, 0, (0, 0), 5), (0, 0, (0, 0), 4)]
        MOD_POOL = [(0, 14), (0, 15), (0, 16), (0, 17)]
        in_blocks = [0, 512, 1024, 1536, 2048, 2560, 3072, 3592, 4104, 4616, 5128]

        def pieces_of_matrix(w, blocks, kt=KT):
            return [(kn(w, k0, 4, c0, BLK), 4) for c0 in blocks for k0 in range(0, kt, 4)]

        pool_pieces = [(d["pool_w"].rearrange("g (k p) n -> p (g k) n", p=P), 8)]
        qkv_pieces = pieces_of_matrix(d["diff_w_qkv"], range(0, 3 * D, BLK))
        wo_pieces = pieces_of_matrix(d["diff_w_o"], (0, BLK))
        in_pieces = pieces_of_matrix(d["w_in_2"][0], in_blocks)
        pa_pieces = pieces_of_matrix(d["w_proj_a_2"][0], (0, BLK), 4)
        pb_pieces = pieces_of_matrix(d["w_proj_b_2"][0], (0, BLK), 4)
        out_pieces = pieces_of_matrix(d["w_out_2"][0], (0, BLK))

        def slot(buf, n, size):
            s = n.first % size
            return buf[:, s * PIECE:(s + 1) * PIECE]

        TURN = {"piece": 6, A: 2, B: 2, T: 2, "step": 2}

        def per_turn(f):
            n = sum(MOD_LOOP[f][2])
            return {**TURN, M: n, "chunk": n, "acc": 8 * n}

        block = ctx.enter_context(nc.Block())


        class Chain:

            def __init__(self, eng, s):
                self.eng, self.s, self.n = eng, s, 0

            def link(self, ins):
                ins.then_inc(self.s, 1)
                self.n += 1

            def wait(self):
                self.eng.wait_ge(self.s, self.n)

        def broadcast(row, n):
            return row.rearrange("(a n) -> a n", a=1).to_broadcast([P, n])

        @block.sync
        def _(sp):
            n = Tally()

            def free_slot(p):
                if p.i is not None or p.first >= RAW:
                    sp.wait_ge(w_hi, p.back(RAW - 2))
                    sp.wait_ge(w_lo, p.back(RAW - 2))
                s = p.first % RAW
                return raw[:, s * PIECE:(s + 1) * PIECE], raw_landed[s]

            def load_gu(w, j, k0):
                dst, landed = free_slot(n.next("piece"))
                dst = dst.rearrange("p (k g n) -> p k g n", k=4, g=2)
                src = w.rearrange("(k p) (g n) -> p k g n", p=P, g=2)
                for g in range(2):
                    sp.dma_start(dst[:, :, g, :], src[:, k0:k0 + 4, g, bass.ds(j * FFW, FFW)]).then_inc(landed, 16)

            def load_down(w, j):
                dst, landed = free_slot(n.next("piece"))
                dst = dst.rearrange("p (k n) -> p k n", k=2)
                src = w.rearrange("(j k p) n -> p k j n", p=P, k=2)
                for k in range(2):
                    sp.dma_start(dst[:, k, :], src[:, k, bass.ds(j, 1), :].rearrange("p j n -> p (j n)"))\
                      .then_inc(landed, 16)

            def ffn(f):
                gu, down = ffns[f]
                load_gu(gu, 0, 0)
                load_gu(gu, 0, 4)
                with sp.Fori(0, (STEPS - 1) // 2) as i:
                    n.enter(i, {"piece": 6})
                    for e in range(2):
                        load_gu(gu, i * 2 + (e + 1), 0)
                        load_gu(gu, i * 2 + (e + 1), 4)
                        load_down(down, i * 2 + e)
                    n.leave((STEPS - 1) // 2)
                load_down(down, STEPS - 1)

            def matrix(pieces):
                for src, k in pieces:
                    dst, landed = free_slot(n.next("piece"))
                    dst = dst.rearrange("p (k n) -> p k n", k=k)
                    for h in range(2):
                        sp.dma_start(dst[:, h * k // 2:(h + 1) * k // 2, :],
                                     src[:, h * k // 2:(h + 1) * k // 2, :]).then_inc(landed, 16)

            sp.dma_start(cact[:, :], d["c_cols"]).then_inc(c_landed, 16)
            sp.dma_start(prow[0:48, :], d["norm_g"].rearrange("l j (k p) -> (l j k) p", p=P)).then_inc(prm_landed, 16)
            sp.dma_start(prow[48:56, :], d["c"].rearrange("a (k p) -> (a k) p", p=P)).then_inc(prm_landed, 16)
            sp.dma_start(prow[56:64, :], d["norm_mix_g_2"].rearrange("a (k p) -> (a k) p", p=P)).then_inc(prm_landed, 16)
            sp.dma_start(prow[64:72, :], d["norm_ffn_g_2"].rearrange("a (k p) -> (a k) p", p=P)).then_inc(prm_landed, 16)
            sp.dma_start(prow[72:104, :], d["conv_w_2"].rearrange("a j (k p) -> (a j k) p", p=P)).then_inc(prm_landed, 16)
            for l in range(2):
                sp.dma_start(brow[l], d["mod_b"][l, :].rearrange("(k p) -> k p", p=P)).then_inc(prm_landed, 16)
            sp.dma_start(ident[:, :], d["ident"]).then_inc(ident_landed, 16)
            sp.dma_start(x, d["x"][0].rearrange("(t p) n -> p t n", p=P)).then_inc(x_landed, 16)
            ffn(0)
            matrix(pool_pieces)
            ffn(1)
            ffn(2)
            matrix(qkv_pieces)
            matrix(wo_pieces)
            ffn(3)
            matrix(in_pieces)
            matrix(pa_pieces)
            matrix(pb_pieces)
            matrix(out_pieces)
            ffn(4)
            for t in range(TB):
                sp.wait_ge(y_ready, t + 1)
                sp.dma_start(out[0, t * P:(t + 1) * P, :], xnt[:, t, :]).then_inc(out_done, 16)
            sp.wait_ge(out_done, 16 * TB)

        @block.tensor
        def _(pe):
            n = Tally()

            def piece():
                p = n.next("piece")
                pe.wait_ge(w_lo, p.back(-2))
                s = p.first % RING
                return whi[:, s * PIECE:(s + 1) * PIECE], wlo[:, s * PIECE:(s + 1) * PIECE]

            def bank(b):
                f = n.next(b)
                if f.first:
                    pe.wait_ge(drained[b], f.at)
                return ps[:, b, :]

            def three(o, hi, lo, wh, wl, start, stop):
                pe.matmul(o, hi, wh, start=start, stop=False)
                pe.matmul(o, hi, wl, start=False, stop=False)
                return pe.matmul(o, lo, wh, start=False, stop=stop)

            def turned(t, h, first):
                pe.wait_ge(nt_lo, 4 * first + 2 * t + h + 1)

            def columns(kt, first):
                o = [None, None]
                for h in range(kt // 4):
                    wh, wl = piece()
                    wh = wh.rearrange("p (k n) -> p k n", k=4)
                    wl = wl.rearrange("p (k n) -> p k n", k=4)
                    for t in range(TB):
                        if h == 0:
                            o[t] = bank((A, B)[t])
                        if first is not None:
                            turned(t, h, first)
                        for k in range(4):
                            kk = 4 * h + k
                            mm = three(o[t], nth[:, kk, t * P:(t + 1) * P], ntl[:, kk, t * P:(t + 1) * P],
                                       wh[:, k, :], wl[:, k, :], kk == 0, kk == kt - 1)
                        if t == 0 and h == kt // 4 - 1:
                            mm.then_inc(filled[A], 1)
                    mm.then_inc(w_used, 1)

            def sums_free(t, s):
                if s:
                    pe.wait_ge(sums_read[t], s)

            def down(par, start, stop, s=None):
                wh, wl = piece()
                wh = wh.rearrange("p (k h n) -> p k h n", k=2, h=2)
                wl = wl.rearrange("p (k h n) -> p k h n", k=2, h=2)
                for t in range(TB):
                    if start:
                        sums_free(t, s)
                    for h in range(2):
                        for k in range(2):
                            mm = three(ps[:, 2 * t + h, :], hth[:, par, k, t * P:(t + 1) * P],
                                       htl[:, par, k, t * P:(t + 1) * P], wh[:, k, h, :], wl[:, k, h, :],
                                       start and k == 0, stop and k == 1)
                    if stop and t == 0:
                        mm.then_inc(sums_done, 1)
                mm.then_inc(w_used, 1)

            def down_piece():
                wh, wl = piece()
                return (wh.rearrange("p (k h n) -> p k h n", k=2, h=2),
                        wl.rearrange("p (k h n) -> p k h n", k=2, h=2))

            def down_block(w, par, t, stop):
                wh, wl = w
                for h in range(2):
                    for k in range(2):
                        mm = three(ps[:, 2 * t + h, :], hth[:, par, k, t * P:(t + 1) * P],
                                   htl[:, par, k, t * P:(t + 1) * P], wh[:, k, h, :], wl[:, k, h, :],
                                   False, stop and k == 1)
                return mm

            def first_columns(first, turn=True):
                w = []
                for t, b in enumerate((A, B)):
                    if t == 0:
                        turned(0, 1, first)
                        o = bank(A)
                    else:
                        o = bank(B)
                    for h in range(2):
                        if t == 0:
                            w.append(tuple(a.rearrange("p (k n) -> p k n", k=4) for a in piece()))
                        if t == 0 and h == 1 and turn:
                            turn_join((1,))
                        turned(t, h, first)
                        for k in range(4):
                            kk = 4 * h + k
                            mm = three(o, nth[:, kk, t * P:(t + 1) * P], ntl[:, kk, t * P:(t + 1) * P],
                                       w[h][0][:, k, :], w[h][1][:, k, :], kk == 0, kk == KT - 1)
                        if t:
                            mm.then_inc(w_used, 1)
                        elif h:
                            mm.then_inc(filled[A], 1)

            def turn_inner():
                pe.wait_ge(drained[A], n.seen(A))
                pe.wait_ge(drained[B], n.seen(B))
                o = bank(T)
                for k in range(2):
                    for t in range(TB):
                        mm = pe.transpose(o[:, (2 * k + t) * P:(2 * k + t + 1) * P],
                                          sil[:, t, k * P:(k + 1) * P], ident[:, :])
                mm.then_inc(filled[T], 1)

            def sum_chunk():
                c = n.next("chunk")
                pe.wait_ge(acc_step, c.at * KT + KT)
                o = bank(M)
                for q in range(MCH // P):
                    mm = pe.matmul(o[:, q:q + 1], acc[:, q * P:(q + 1) * P], ones[:, 0:1], start=True, stop=True)
                mm.then_inc(filled[M], 1)

            def own_chunk(lap):
                o = bank(M)
                for k in range(KT):
                    if k % 4 == 0:
                        pe.wait_ge(first_landed[k // 4], 16 * lap)
                    mm = pe.matmul(o[0:1, :], cact[:, k:k + 1], mfirst[k // 4][:, k % 4, :],
                                   start=(k == 0), stop=(k == KT - 1))
                    if k == 3:
                        mm.then_inc(first_used, 1)
                mm.then_inc(filled[M], 1)
                o = bank(M)
                for q in range(MCH // P):
                    mm = pe.matmul(o[:, q:q + 1], gate[0:1, q * P:(q + 1) * P], ones[0:1, 0:1], start=True, stop=True)
                mm.then_inc(filled[M], 1)

            def gate_rows():
                g = n.next("gate")
                pe.wait_ge(diag_ready, g.at + 1)
                for h, b in enumerate((M, T)):
                    pe.matmul(bank(b), ones[:, :], xn[:, h * BLK:(h + 1) * BLK], start=True, stop=True)\
                      .then_inc(filled[b], 1)

            def turn_join(blocks=(0, 1)):
                for t in blocks:
                    j = n.next("join")
                    pe.wait_ge(rdiag_ready, j.at + 1)
                    for h in range(2):
                        turn_half(x, t, h, rdiag[:, t * P:(t + 1) * P])

            def turn_half(src, t, h, times=None):
                b = ((A, B), (T, M))[t][h]
                o = bank(b)
                for q in range(4):
                    tile = src[:, t, (4 * h + q) * P:(4 * h + q + 1) * P]
                    if times is None:
                        mm = pe.transpose(o[:, q * P:(q + 1) * P], tile, ident[:, :])
                    else:
                        mm = pe.matmul(o[:, q * P:(q + 1) * P], tile, times, start=True, stop=True)
                mm.then_inc(filled[b], 1)

            def ffn(f, gated):
                first, s = n.next("turned").at, n.next("sums").at
                first_columns(first)
                turn_inner()
                def step(par, start):
                    columns(KT, None)
                    pe.wait_ge(drained[T], n.seen(T))
                    down(1 - par, start, False, s)
                    turn_inner()
                step(1, True)
                if MOD_LOOP[f][2][0]:
                    sum_chunk()
                turns = min(MOD_LOOP[f][3], 5) - 1 if f != 4 else (STEPS - 3) // 2
                with pe.Fori(0, turns) as i:
                    n.enter(i, pe_turn(f))
                    for e in range(2):
                        step(e, False)
                        if MOD_LOOP[f][2][1 - e]:
                            sum_chunk()
                    n.leave(turns)
                if turns < (STEPS - 3) // 2:
                    step(0, False)
                    sum_chunk()
                    step(1, False)
                columns(KT, None)
                pe.wait_ge(drained[T], n.seen(T))
                before = down_piece()
                down_block(before, 1, 0, False)
                turn_inner()
                if MOD_LOOP[f][2][1] and MOD_LOOP[f][3] == 5:
                    sum_chunk()
                if gated:
                    gate_rows()
                    pe.wait_ge(drained[T], n.seen(T) - 1)
                else:
                    pe.wait_ge(drained[T], n.seen(T))
                last = down_piece()
                down_block(last, 0, 0, True).then_inc(sums_done, 1)
                down_block(before, 1, 1, False).then_inc(w_used, 1)
                down_block(last, 0, 1, True).then_inc(w_used, 1)

            def pe_turn(f):
                k = sum(MOD_LOOP[f][2])
                return {"piece": 6, A: 2, B: 2, T: 2, **({M: k, "chunk": k} if k else {})}

            def pool():
                for j in range(4):
                    own_chunk(3 + j)
                gate_rows()
                wh, wl = piece()
                wh = wh.rearrange("p (k n) -> p k n", k=KT)
                wl = wl.rearrange("p (k n) -> p k n", k=KT)
                s = n.next("sums").at
                for t in range(TB):
                    sums_free(t, s)
                    for g in range(4):
                        pe.wait_ge(pool_lo, g + 1)
                        o = ps[:, 2 * t + g // 2, (g % 2) * 256:(g % 2) * 256 + 256]
                        for k in (2 * g, 2 * g + 1):
                            mm = three(o, nth[:, k, t * P:(t + 1) * P], ntl[:, k, t * P:(t + 1) * P],
                                       wh[:, k, :], wl[:, k, :], k == 2 * g, k == 2 * g + 1)
                    if t == 0:
                        mm.then_inc(sums_done, 1)
                mm.then_inc(w_used, 1)

            def onto_sums(halves, first, k0=0):
                s = n.next("sums").at
                for c in range(2):
                    for h in range(halves):
                        wh, wl = piece()
                        wh = wh.rearrange("p (k n) -> p k n", k=4)
                        wl = wl.rearrange("p (k n) -> p k n", k=4)
                        for t in range(TB):
                            if c == 0 and h == 0:
                                sums_free(t, s)
                            turned(t, (k0 + 4 * h) // 4, first)
                            for k in range(4):
                                kk = k0 + 4 * h + k
                                mm = three(ps[:, 2 * t + c, :], nth[:, kk, t * P:(t + 1) * P],
                                           ntl[:, kk, t * P:(t + 1) * P], wh[:, k, :], wl[:, k, :],
                                           h == 0 and k == 0, h == halves - 1 and k == 3)
                            if c == 1 and h == halves - 1 and t == 0:
                                mm.then_inc(sums_done, 1)
                        mm.then_inc(w_used, 1)

            def diff_attention():
                first = n.next("turned").at
                first_columns(first)
                for _ in range(5):
                    columns(KT, first)
                pe.wait_ge(roped, 2)
                pe.wait_ge(drained[A], n.seen(A))
                pe.wait_ge(drained[B], n.seen(B))

                def turn_qk(h):
                    o = bank(T)
                    for i, c0 in enumerate((0, D)):
                        for t in range(TB):
                            mm = pe.transpose(o[:, (2 * i + t) * P:(2 * i + t + 1) * P],
                                              qkv[:, t, c0 + h * P:c0 + (h + 1) * P], ident[:, :])
                    mm.then_inc(filled[T], 1)

                def scores(h):
                    pe.wait_ge(drained[T], n.seen(T))
                    for c, b in enumerate((A, B)):
                        o = bank(b)
                        rows = slice(64 * c, 64 * c + 64)
                        for t in range(TB):
                            mm = pe.matmul(o[:, t * S:(t + 1) * S], qkT[rows, h % 2, t * P:(t + 1) * P],
                                           qkT[rows, h % 2, S:2 * S], start=True, stop=True)
                        mm.then_inc(filled[b], 1)

                def turn_weights(h):
                    pe.wait_ge(mix_ready, 2 * h + 2)
                    o = bank(M)
                    for t in range(TB):
                        for k in range(TB):
                            mm = pe.transpose(o[:, (2 * t + k) * P:(2 * t + k + 1) * P],
                                              av[:, t, k * P:(k + 1) * P], ident[:, :])
                    mm.then_inc(filled[M], 1)

                def mix(h):
                    pe.wait_ge(drained[M], n.seen(M))
                    if h >= 2:
                        pe.wait_ge(out_copied, h - 1)
                    for t in range(TB):
                        for k in range(TB):
                            mm = pe.matmul(ps[:, 2 * (h % 2), t * P:(t + 1) * P], avT[:, t, k, :],
                                           qkv[:, k, 2 * D + h * P:2 * D + (h + 1) * P],
                                           start=(k == 0), stop=(k == 1))
                    mm.then_inc(head_out, 1)

                for h in range(H1 + 1):
                    if h < H1:
                        turn_qk(h)
                    if h:
                        turn_weights(h - 1)
                    if h < H1:
                        scores(h)
                    if h:
                        mix(h - 1)
                gate_rows()
                pe.wait_ge(heads_normed, 2)
                for t in range(TB):
                    for h in range(2):
                        turn_half(qkv, t, h)
                onto_sums(2, n.next("turned").at)

            def second_mix(turn):
                first = n.next("turned").at
                pe.wait_ge(mix_landed, 16 * 4)
                o = bank(M)
                for t in range(TB):
                    for k in range(KT):
                        mm = pe.matmul(o[:, 8 * t:8 * t + 8], xnt[:, t, k * P:(k + 1) * P], w8[:, k, :],
                                       start=(k == 0), stop=(k == KT - 1))
                mm.then_inc(filled[M], 1)
                first_columns(first, turn)
                for b in range(2):
                    columns(KT, first)
                for b in range(2):
                    columns(KT, first)
                    pe.wait_ge(conv_in, 2 * b + 2)
                    for t in range(TB):
                        o = bank((T, M)[t])
                        for q in range(4):
                            mm = pe.transpose(o[:, q * P:(q + 1) * P], convin[:, t, q * P:(q + 1) * P], ident[:, :])
                        mm.then_inc(filled[(T, M)[t]], 1)
                for b in range(2):
                    columns(KT, first)

                def gate_columns(j, h, t, w):
                    if h == 0 and t == 0 and j >= 2:
                        pe.wait_ge(gab_read, j - 1)
                    for k in range(4):
                        kk = 4 * h + k
                        mm = three(ps[:, 2 * t + j % 2, :], nth[:, kk, t * P:(t + 1) * P],
                                   ntl[:, kk, t * P:(t + 1) * P], w[0][:, k, :], w[1][:, k, :],
                                   kk == 0, kk == KT - 1)
                    if t:
                        mm.then_inc(w_used, 1)

                pe.wait_ge(roped, 4)
                pe.wait_ge(conv_done, 8)
                def turn_pair(r):
                    o = bank(T)
                    for i, c0 in enumerate((0, 512)):
                        for t in range(TB):
                            mm = pe.transpose(o[:, (2 * i + t) * P:(2 * i + t + 1) * P],
                                              qkva[:, t, c0 + r * P:c0 + (r + 1) * P], ident[:, :])
                    mm.then_inc(filled[T], 1)

                def scores(h):
                    pe.wait_ge(drained[T], n.seen(T))
                    rows = slice(64 * (h % 2), 64 * (h % 2) + 64)
                    o = bank(A)
                    pe.matmul(o[:, 0:P], qTa[rows, 0:P], kTa[rows, 0:P], start=True, stop=True)
                    pe.matmul(o[:, P:3 * P], qTa[rows, P:S], kTa[rows, 0:S], start=True, stop=True)\
                      .then_inc(filled[A], 1)

                def turn_probs(h):
                    pe.wait_ge(probs_ready, h + 1)
                    o = bank(M)
                    for q in range(3):
                        mm = pe.transpose(o[:, q * P:(q + 1) * P], pa2[h % 2][:, q * P:(q + 1) * P], ident[:, :])
                    mm.then_inc(filled[M], 1)

                def times_v(h):
                    pe.wait_ge(drained[M], n.seen(M))
                    o = bank(B)
                    v = qkva[:, :, 1024 + h * 64:1024 + (h + 1) * 64]
                    pe.matmul(o[:, 0:64], paT[:, 0:P], v[:, 0, :], start=True, stop=True)
                    pe.matmul(o[:, 64:128], paT[:, P:2 * P], v[:, 0, :], start=True, stop=False)
                    pe.matmul(o[:, 64:128], paT[:, 2 * P:3 * P], v[:, 1, :], start=False, stop=True)\
                      .then_inc(filled[B], 1)

                for h in range(HA + 1):
                    if h < HA:
                        if h % 2 == 0 and h:
                            turn_pair(h // 2)
                        w = tuple(a.rearrange("p (k n) -> p k n", k=4) for a in piece())
                        gate_columns(h // 2, h % 2, 0, w)
                        if h == 0:
                            pe.wait_ge(ob_scaled, 1)
                            turn_pair(0)
                        scores(h)
                    if h:
                        turn_probs(h - 1)
                    if h < HA:
                        gate_columns(h // 2, h % 2, 1, w)
                    if h:
                        times_v(h - 1)

                pe.wait_ge(gated, 1)
                pe.wait_ge(drained[B], n.seen(B))
                o = bank(T)
                for g in range(2):
                    for t in range(TB):
                        mm = pe.transpose(o[0:4, (2 * g + t) * P:(2 * g + t + 1) * P],
                                          small[:, 8 * t + 4 * g:8 * t + 4 * g + 4], ident[:, :])
                mm.then_inc(filled[T], 1)
                pe.wait_ge(rows_done, 1)
                o = bank(M)
                for g, src in enumerate((va_rows[3], va_rows[1])):
                    for t in range(TB):
                        mm = pe.transpose(o[:, (2 * g + t) * 4:(2 * g + t) * 4 + 4], src[:, t * P:(t + 1) * P],
                                          ident[0:4, 0:4])
                mm.then_inc(filled[M], 1)
                pe.wait_ge(late_landed, 32)
                def decay_scores(h):
                    o = bank(T)
                    pe.matmul(o[:, 0:S], pick[:, h * P:(h + 1) * P], va_rows[0], start=True, stop=True)\
                      .then_inc(filled[T], 1)
                    if h:
                        pe.wait_ge(drained[A], n.seen(A))
                    o = bank(A)
                    q, k = qkc[:, h, :], qkc[:, 4 + h, :]
                    pe.matmul(o[:, 0:S], k[:, 0:P], q, start=True, stop=True)
                    pe.matmul(o[:, S:S + P], k[:, P:S], q[:, P:S], start=True, stop=True).then_inc(filled[A], 1)

                for h in range(HB):
                    if h == 0:
                        decay_scores(h)
                    if h + 1 < HB:
                        decay_scores(h + 1)
                    else:
                        pe.wait_ge(drained[A], n.seen(A))
                    o = bank(B)
                    pe.matmul(o[:, 0:129], scT[:, 0:P], vbx[:, 0, h, :], start=True, stop=True)
                    pe.matmul(o[:, 129:258], scT[:, P:S], vbx[:, 0, h, :], start=True, stop=False)
                    pe.matmul(o[:, 129:258], scT[:, S:S + P], vbx[:, 1, h, :], start=False, stop=True)\
                      .then_inc(filled[B], 1)
                pe.wait_ge(y_done, 1)
                for t in range(TB):
                    for h in range(2):
                        turn_half(qkva, t, h)
                first = n.next("turned").at
                pe.wait_ge(gab_read, 4)
                onto_sums(1, first, 0)
                for c in range(2):
                    for_b(first)
                pe.wait_ge(merged, 2)
                for t in range(TB):
                    for h in range(2):
                        turn_half(xnt, t, h)
                onto_sums(2, n.next("turned").at)

            def for_b(first):
                wh, wl = piece()
                wh = wh.rearrange("p (k n) -> p k n", k=4)
                wl = wl.rearrange("p (k n) -> p k n", k=4)
                for t in range(TB):
                    o = bank((A, B)[t])
                    turned(t, 1, first)
                    for k in range(4):
                        mm = three(o, nth[:, 4 + k, t * P:(t + 1) * P], ntl[:, 4 + k, t * P:(t + 1) * P],
                                   wh[:, k, :], wl[:, k, :], k == 0, k == 3)
                    if t == 0:
                        mm.then_inc(filled[A], 1)
                mm.then_inc(w_used, 1)

            pe.sem_inc(w_used, 1)
            pe.wait_ge(prm_landed, 16 * 7)
            pe.wait_ge(ident_landed, 16)
            o = bank(A)
            pe.transpose(o[:, 0:NROWS], prow[0:NROWS, :], ident[0:NROWS, 0:NROWS])
            pe.transpose(o[:, 128:200], brow[0][:, :], ident[0:72, 0:72])
            pe.transpose(o[:, 256:328], brow[1][:, :], ident[0:72, 0:72]).then_inc(filled[A], 1)
            pe.wait_ge(consts_set, 3)
            pe.wait_ge(cact_ready, 1)
            for j in range(2):
                own_chunk(j + 1)
                sum_chunk()
            turn_join((0,))
            ffn(0, True)
            turn_join()
            pool()
            turn_join((0,))
            ffn(1, True)
            turn_join((0,))
            ffn(2, True)
            turn_join((0,))
            diff_attention()
            turn_join((0,))
            ffn(3, True)
            turn_join()
            second_mix(False)
            turn_join((0,))
            ffn(4, False)

        @block.scalar
        def _(act):
            n = Tally()
            own = Chain(act, act_chain)

            def make_hi():
                p = n.next("piece")
                act.wait_ge(raw_landed[p.first % RAW], p.lap(RAW) * 32 + 32)
                if p.i is not None or p.first >= RING:
                    act.wait_ge(w_used, p.back(RING - 2))
                s, r = p.first % RING, p.first % RAW
                nc.scalar.activation(whi[:, s * PIECE:(s + 1) * PIECE], raw[:, r * PIECE:(r + 1) * PIECE],
                                     ACT.Copy).then_inc(w_hi, 1)

            def split(k):
                for _ in range(k):
                    make_hi()

            def full(b):
                f = n.next(b)
                act.wait_ge(filled[b], (n.next("small B") if b == B else f).at + 1)
                return ps[:, b, :]

            def full_with_piece(b, pieces_behind):
                n.next(b)
                act.wait_ge(w_used, n.seen("piece") - (pieces_behind - 1))
                return ps[:, b, :]

            def inner():
                f = n.next(A)
                act.wait_ge(filled[A], f.at + 1)
                nc.scalar.activation(sil[:, 0, :], ps[:, A, 0:FFW], ACT.Silu).then_inc(silu_done, 1)

            def steps(f, k, ahead):
                split(ahead)
                inner()
                full_with_piece(B, k)
                nc.scalar.activation(sil[:, 1, :], ps[:, B, 0:FFW], ACT.Silu).then_inc(silu_done, 1)

            def inner_hi(par):
                o = full(T)
                nc.scalar.activation(hthi[:, par * BLK:(par + 1) * BLK], o, ACT.Copy).then_inc(ht_hi, 1)

            def step(par, k, ahead=3):
                steps(None, k, ahead)
                inner_hi(par)

            def gate_rows(scale):
                g = n.next("gate")
                if g.first:
                    act.wait_ge(gate_used, 2 * g.at)
                for h, b in enumerate((M, T)):
                    o = full(b)
                    nc.scalar.activation(gate[:, h * BLK:(h + 1) * BLK], o, ACT.Copy, scale=scale)\
                      .then_inc(drained[b], 1)

            def squares(t):
                q = n.next("squares")
                act.wait_ge(x_ready, q.at + 1)
                junk = ps[:, (A, T)[t]:(A, T)[t] + 2, :].rearrange("p b n -> p (b n)")
                nc.scalar.activation(junk, x[:, t, :], ACT.Square, accum_out=ss[:, t:t + 1]).then_inc(sq_done, 1)

            def join(g_cols, shift=None, split_too=True, squared=1):
                for t in range(TB):
                    for _ in range(squared):
                        squares(t)
                for t in range(TB):
                    for h in range(2):
                        b = ((A, B), (T, M))[t][h]
                        if h == 1:
                            o = full(b)
                            if t == 0:
                                act.wait_ge(g_ready, n.next("g").at + 1)
                            for q in range(4):
                                k = 4 + q
                                e = nc.scalar.activation(xnt[:, t, k * P:(k + 1) * P], o[:, q * P:(q + 1) * P],
                                                         ACT.Identity, scale=g_cols[:, k:k + 1],
                                                         bias=0.0 if shift is None else shift[:, k:k + 1])
                            e.then_inc(drained[b], 1)
                            bn = n.seen(b)
                        else:
                            n.next(b)
                            bn = n.seen(b)
                        if split_too:
                            act.wait_ge(drained[b], bn)
                            nc.scalar.activation(nth[:, 4 * h:4 * h + 4, t * P:(t + 1) * P],
                                                 xnt[:, t, h * BLK:(h + 1) * BLK].rearrange("p (k s) -> p k s", k=4),
                                                 ACT.Copy).then_inc(nt_hi, 1)

            def turned_hi():
                for t in range(TB):
                    for h in range(2):
                        o = full(((A, B), (T, M))[t][h])
                        nc.scalar.activation(nth[:, 4 * h:4 * h + 4, t * P:(t + 1) * P],
                                             o.rearrange("p (k s) -> p k s", k=4), ACT.Copy).then_inc(nt_hi, 1)

            def skip_chunks(k):
                for _ in range(k):
                    n.next(M)

            def keep_row():
                o = full(M)
                nc.scalar.activation(gate[0:1, 0:BLK], o[0:1, :], ACT.Copy).then_inc(drained[M], 1)
                n.next(M)

            def ffn(f, gated):
                step(0, 1, 1)
                split(2)
                pat, turns = MOD_LOOP[f][2:]
                with act.Fori(0, turns) as i:
                    n.enter(i, {"piece": 6, A: 2, B: 2, T: 2, **({M: sum(pat)} if sum(pat) else {})})
                    for e in range(2):
                        step(1 - e, 4)
                        skip_chunks(pat[e])
                    n.leave(turns)
                if f == 4:
                    step(1, 4)
                    step(0, 2, 1)
                elif turns < 5:
                    step(1, 4)
                    step(0, 4)
                if gated:
                    gate_rows(0.5)

            def pool():
                for g in range(4):
                    act.wait_ge(pool_diff, g + 1)
                    src = win[(g + 1) % 2][:, :, 8:8 + S]
                    nc.scalar.activation(nth[:, 2 * g:2 * g + 2, :], src, ACT.Copy).then_inc(pool_hi, 1)
                    keep_row()
                gate_rows(1.0)
                split(1)

            def diff_attention():
                for b in range(6):
                    split(2)
                    f = n.next(A)
                    act.wait_ge(filled[A], f.at + 1)
                    nc.scalar.activation(qkv[:, 0, b * BLK:(b + 1) * BLK], ps[:, A, :], ACT.Copy)\
                      .then_inc(drained[A], 1)
                    n.next(B)
                act.wait_ge(lam_prod, 1)
                nc.scalar.activation(lam[:, 2:4], lam[:, 0:2], ACT.Exp).then_inc(lam_exp, 1)

                def turned_qk(h):
                    o = full(T)
                    nc.scalar.activation(qkT[:, h % 2, 0:S], o[:, 0:S], ACT.Copy, scale=HD1 ** -0.5)
                    nc.scalar.activation(qkT[:, h % 2, S:2 * S], o[:, S:2 * S], ACT.Copy).then_inc(drained[T], 1)

                def exps(h):
                    if h:
                        act.wait_ge(mix_ready, 2 * h)
                    for c, b in enumerate((A, B)):
                        act.wait_ge(top_ready, 2 * h + c + 1)
                        o = full(b)
                        for t in range(TB):
                            i = 2 * c + t
                            e = nc.scalar.activation(pr[:, c, t, :], o[:, t * S:(t + 1) * S], ACT.Exp,
                                                     bias=top[:, i:i + 1], accum_out=total[:, i:i + 1])
                            if t:
                                e.then_inc(drained[b], 1)

                def weights(h):
                    o = full(M)
                    nc.scalar.activation(avT.rearrange("p t k q -> p (t k q)"), o, ACT.Copy).then_inc(drained[M], 1)

                def mixed(h):
                    act.wait_ge(head_out, h + 1)
                    b = 2 * (h % 2)
                    nc.scalar.activation(qkv[:, :, h * P:(h + 1) * P],
                                         ps[:, b, 0:S].rearrange("p (t n) -> p t n", t=TB), ACT.Copy)
                    for t in range(TB):
                        e = nc.scalar.activation(ps[:, b + 1, t * P:(t + 1) * P], ps[:, b, t * P:(t + 1) * P],
                                                 ACT.Square, accum_out=hss[:, 8 * t + h:8 * t + h + 1])
                    e.then_inc(out_copied, 1)

                for h in range(H1 + 1):
                    if h < H1:
                        turned_qk(h)
                    if h:
                        weights(h - 1)
                    if h < H1:
                        exps(h)
                    if h:
                        mixed(h - 1)
                gate_rows(1.0)
                turned_hi()
                split(4)

            def second_mix():
                n.next(M)
                for b in range(3):
                    split(2)
                    o = full(A)
                    nc.scalar.activation(qkva[:, 0, b * BLK:(b + 1) * BLK], o, ACT.Copy).then_inc(drained[A], 1)
                    n.next(B)
                for b in range(2):
                    split(2)
                    o = full(A)
                    if b:
                        act.wait_ge(filled[M], n.seen(M))
                    nc.scalar.activation(convin[:, 0, :], o, ACT.Copy).then_inc(conv_in, 1)
                    n.next(B)
                    n.next(T)
                    n.next(M)
                    for q in range(4):
                        act.wait_ge(conv_sum, 4 * b + q + 1)
                        nc.scalar.activation(qkc[:, 4 * b + q, :], qkc[:, 4 * b + q, :], ACT.Silu)\
                          .then_inc(conv_out, 1)
                split(2)
                o = full(A)
                nc.scalar.activation(vbx[:, 0, :, 0:P], o.rearrange("p (h n) -> p h n", h=HB), ACT.Copy)\
                  .then_inc(drained[A], 1)
                n.next(B)
                split(2)
                for t in range(TB):
                    o = full(A) if t == 0 else full_with_piece(B, 2)
                    nc.scalar.activation(obt[:, t, :], o, ACT.Sigmoid).then_inc(drained[(A, B)[t]], 1)
                pieces_before = n.seen("piece") - 2

                def keep_gates(j):
                    act.wait_ge(w_used, 1 + pieces_before + 2 * (j + 1))
                    for t in range(TB):
                        dst = gab2[:, t, :] if j == 3 else gab[:, t, j * BLK:(j + 1) * BLK]
                        e = nc.scalar.activation(dst, ps[:, 2 * t + j % 2, :], ACT.Copy)
                    e.then_inc(gab_read, 1)

                for h in range(HA + 1):
                    if h < HA and h % 2 == 0:
                        o = full(T)
                        nc.scalar.activation(qTa, o[:, 0:S], ACT.Copy, scale=HDA ** -0.5)
                        nc.scalar.activation(kTa, o[:, S:2 * S], ACT.Copy).then_inc(drained[T], 1)
                    if h:
                        e = h - 1
                        c, p = 2 * (e % 2), pa2[e % 2]
                        n.next(A)
                        act.wait_ge(top_ready, 2 * H1 + e + 1)
                        nc.scalar.activation(p[:, 0:P], p[:, 0:P], ACT.Exp, bias=top[:, c:c + 1],
                                             accum_out=total[:, c:c + 1])
                        nc.scalar.activation(p[:, P:3 * P], p[:, P:3 * P], ACT.Exp, bias=top[:, c + 1:c + 2],
                                             accum_out=total[:, c + 1:c + 2]).then_inc(probs_ready, 1)
                        o = full(M)
                        nc.scalar.activation(paT, o[:, 0:3 * P], ACT.Copy).then_inc(drained[M], 1)
                        n.next(B)
                        n.next("small B")
                    if h < HA:
                        split(1)
                    if h % 2 == 0 and h:
                        keep_gates(h // 2 - 1)
                split(2)

                n.next(T)
                act.wait_ge(filled[T], n.seen(T))
                own.link(nc.scalar.activation(va_rows[0], ps[0:4, T, S:2 * S], ACT.Abs))
                own.wait()
                own.link(nc.scalar.activation(va_rows[0], va_rows[0], ACT.Exp, scale=-1.0))
                own.wait()
                nc.scalar.activation(va_rows[0], va_rows[0], ACT.Ln, bias=1.0).then_inc(rows_act, 1)
                act.wait_ge(rows_step, 1)
                nc.scalar.activation(va_rows[1], va_rows[1], ACT.Exp, scale=-1.0).then_inc(rows_done, 1)
                n.next(M)
                for h in range(HB):
                    n.next(T)
                    n.next(A)
                    for e in ((0, 1), (2,), (3,), ())[h]:
                        act.wait_ge(decay_in, e + 1)
                        nc.scalar.activation(decay, decay, ACT.Exp, scale=-1.0).then_inc(decay_out, 1)
                    o = full(B)
                    if h:
                        act.wait_ge(den_ready, 2 * h)
                    nc.scalar.activation(total[:, 0:2], o[:, P:P + 130:129], ACT.Abs).then_inc(den_abs, 1)
                    for t in range(TB):
                        act.wait_ge(den_ready, 2 * h + t + 1)
                        nc.scalar.activation(qkva[:, t, 512 + h * P:512 + (h + 1) * P], o[:, 129 * t:129 * t + P],
                                             ACT.Copy, scale=inv[:, t:t + 1])\
                          .then_inc(hb_ready, 1)
                        act.wait_ge(hb_ready, 2 * h + t + 1)
                        e = nc.scalar.activation(junkh, qkva[:, t, 512 + h * P:512 + (h + 1) * P], ACT.Square,
                                                 accum_out=hss[:, 4 * t + h:4 * t + h + 1])
                    e.then_inc(drained[B], 1)
                act.wait_ge(gab_read, 4)
                nc.scalar.activation(gab, gab, ACT.Sigmoid)
                nc.scalar.activation(gab2, gab2, ACT.Sigmoid).then_inc(gab_ready, 1)
                turned_hi()
                for c in range(2):
                    n.next(A)
                    n.next(B)
                    split(1)
                turned_hi()
                split(4)

            act.sem_inc(w_hi, 1)
            act.wait_ge(c_landed, 16)
            nc.scalar.activation(cact[:, :], cact[:, :], ACT.Silu).then_inc(cact_ready, 1)
            n.next(A)
            split(2)
            for _ in range(2):
                keep_row()
                n.next(M)
            join(scol, mod_cols(0, 0))
            ffn(0, True)
            join(scol, mod_cols(0, 3), split_too=False)
            pool()
            join(scol, mod_cols(0, 6))
            ffn(1, True)
            join(scol, mod_cols(1, 0))
            ffn(2, True)
            join(scol, mod_cols(1, 3))
            diff_attention()
            join(scol, mod_cols(1, 6))
            ffn(3, True)
            join(cols[:, C_MIX:C_MIX + KT], squared=2)
            second_mix()
            join(cols[:, C_FFN:C_FFN + KT])
            ffn(4, False)
            for t in range(TB):
                squares(t)

        @block.vector
        def _(dve):
            n = Tally()
            own = Chain(dve, dve_chain)
            v = nc.vector

            def make_lo():
                p = n.next("piece")
                dve.wait_ge(w_hi, p.back(-2))
                s, r = p.first % RING, p.first % RAW
                hi = whi[:, s * PIECE:(s + 1) * PIECE].bitcast(F32)
                v.tensor_tensor(wlo[:, s * PIECE:(s + 1) * PIECE], raw[:, r * PIECE:(r + 1) * PIECE], hi,
                                ALU.subtract).then_inc(w_lo, 1)

            def split(k):
                for _ in range(k):
                    make_lo()

            def full(b):
                f = n.next(b)
                dve.wait_ge(filled[b], (n.next("small B") if b == B else f).at + 1)
                return ps[:, b, :]

            def full_with_piece(b, pieces_behind):
                n.next(b)
                dve.wait_ge(w_used, n.seen("piece") - (pieces_behind - 1))
                return ps[:, b, :]

            def add_chunk(first=None):
                c = n.next("chunk")
                for k in range(KT):
                    if k % 4 == 0 and first is None:
                        dve.wait_ge(mod_landed[k // 4], c.back(2) * 16 + 16)
                    elif k % 4 == 0:
                        dve.wait_ge(first_landed[2 + k // 4], 16 * first)
                    src = (mraw if first is None else mfirst[2:])[k // 4][:, k % 4, :]
                    if k == 0:
                        e = v.tensor_scalar(acc, src, cact[:, 0:1], None, ALU.mult)
                    else:
                        dve.wait_ge(acc_step, c.at * KT + k)
                        e = v.scalar_tensor_tensor(acc, src, cact[:, k:k + 1], acc, ALU.mult, ALU.add)
                    e.then_inc(acc_step, 1)

            def keep_chunk(at):
                o = full(M)
                v.tensor_tensor(modc[:, bass.ds(at, 4)], o[:, 0:4], modb[:, bass.ds(at, 4)], ALU.add)\
                 .then_inc(drained[M], 1)

            def keep_own_chunk(at):
                n.next(M)
                keep_chunk(at)

            def chunk_at(layer, chunk):
                return layer * NMOD * KT + chunk * 4

            def inner(k, ahead=3):
                for t, b in enumerate((A, B)):
                    if t == 0:
                        f = n.next(A)
                        s = n.next("silu")
                    else:
                        full_with_piece(B, k)
                        s = n.next("silu")
                    dve.wait_ge(silu_done, s.at + 1)
                    v.tensor_tensor(sil[:, t, :], sil[:, t, :], ps[:, b, FFW:2 * FFW], ALU.mult)\
                     .then_inc(drained[b], 1)

            def inner_lo(par):
                f = n.next(T)
                dve.wait_ge(ht_hi, n.next("inner").at + 1)
                at = slice(par * BLK, (par + 1) * BLK)
                v.tensor_tensor(htlo[:, at], ps[:, T, :], hthi[:, at].bitcast(F32), ALU.subtract)\
                 .then_inc(drained[T], 1)

            def ffn(f, gated):
                split(1)
                inner(1)
                inner_lo(0)
                split(2)
                layer, first, pat, turns = MOD_LOOP[f]
                per = sum(pat)
                with dve.Fori(0, turns) as i:
                    n.enter(i, {"piece": 6, A: 2, B: 2, T: 2, "silu": 4, "inner": 2,
                                **({M: per, "chunk": per} if per else {})})
                    k = 0
                    for e in range(2):
                        split(3)
                        if pat[e]:
                            add_chunk()
                        inner(4)
                        inner_lo(1 - e)
                        if pat[e]:
                            keep_chunk(i * (4 * per) + (chunk_at(layer, first) + 4 * k))
                            k += 1
                    n.leave(turns)
                if f == 4:
                    split(3)
                    inner(4)
                    inner_lo(1)
                    split(1)
                    inner(2)
                    inner_lo(0)
                elif turns < 5:
                    for e in range(2):
                        split(3)
                        inner(4)
                        inner_lo(1 - e)
                if gated:
                    n.next(M)
                    n.next(T)

            def joined(t, gated, by_piece):
                s = n.next("sums 0") if t == 0 else n.next("sums 1")
                if t == 0:
                    dve.wait_ge(sums_done, s.at + 1)
                else:
                    dve.wait_ge(w_used, n.seen("piece") - (by_piece - 1))
                o = ps[:, 2 * t:2 * t + 2, :].rearrange("p b n -> p (b n)")
                if gated:
                    if t == 0:
                        dve.wait_ge(drained[M], n.seen(M))
                        dve.wait_ge(drained[T], n.seen(T))
                    v.tensor_tensor(xnt[:, t, :], o, gate[:, :], ALU.mult).then_inc(sums_read[t], 1)
                    dve.wait_ge(sums_read[t], s.at + 1)
                    v.engine_nop().then_inc(gate_used, 1)
                    own.link(v.tensor_tensor(x[:, t, :], x[:, t, :], xnt[:, t, :], ALU.add))
                else:
                    v.tensor_tensor(x[:, t, :], x[:, t, :], o, ALU.add).then_inc(sums_read[t], 1)
                    dve.wait_ge(sums_read[t], s.at + 1)

            def join(g_cols, shift=None, scale=None, sums=True, gated=True, by_piece=2, split_too=True,
                     final=False):
                if scale is not None:
                    own.link(v.scalar_tensor_tensor(scol[:, :], scale, 1.0, g_cols, ALU.add, ALU.mult))
                    own.wait()
                    g_cols = scol[:, :]
                v.engine_nop().then_inc(g_ready, 1)
                for t in range(TB):
                    if sums:
                        joined(t, gated, by_piece)
                        if gated:
                            own.wait()
                    elif t == 0:
                        dve.wait_ge(x_landed, 16)
                    nx = n.next("x")
                    v.engine_nop().then_inc(x_ready, 1)
                    if final:
                        r, nx = n.next("rstd"), n.next("x")
                        if t == 0:
                            dve.wait_ge(row_landed, 32)
                        dve.wait_ge(rstd_done, r.at + 1)
                        v.scalar_tensor_tensor(x[:, t, :], x[:, t, :], rstd[:, t:t + 1], row, ALU.mult, ALU.mult)\
                         .then_inc(x_ready, 1)
                        dve.wait_ge(x_ready, nx.at + 1)
                    n.next("rstd")
                for t in range(TB):
                    for h in range(2):
                        b = ((A, B), (T, M))[t][h]
                        if h:
                            n.next(b)
                            if b == B:
                                n.next("small B")
                            continue
                        o = full(b)
                        for q in range(4):
                            k = 4 * h + q
                            e = v.tensor_scalar(xnt[:, t, k * P:(k + 1) * P], o[:, q * P:(q + 1) * P],
                                                g_cols[:, k:k + 1], None if shift is None else shift[:, k:k + 1],
                                                ALU.mult, *(() if shift is None else (ALU.add,)))
                        e.then_inc(drained[b], 1)
                    if split_too:
                        for h in range(2):
                            dve.wait_ge(nt_hi, n.next("turned half").at + 1)
                            at = nth[:, 4 * h:4 * h + 4, t * P:(t + 1) * P]
                            v.tensor_tensor(ntl[:, 4 * h:4 * h + 4, t * P:(t + 1) * P],
                                            xnt[:, t, h * BLK:(h + 1) * BLK].rearrange("p (k s) -> p k s", k=4),
                                            at.bitcast(F32), ALU.subtract).then_inc(nt_lo, 1)

            def turned_lo():
                for t in range(TB):
                    for h in range(2):
                        b = ((A, B), (T, M))[t][h]
                        n.next(b)
                        if b == B:
                            n.next("small B")
                        dve.wait_ge(nt_hi, n.next("turned half").at + 1)
                        v.tensor_tensor(ntl[:, 4 * h:4 * h + 4, t * P:(t + 1) * P],
                                        ps[:, b, :].rearrange("p (k s) -> p k s", k=4),
                                        nth[:, 4 * h:4 * h + 4, t * P:(t + 1) * P].bitcast(F32), ALU.subtract)\
                         .then_inc(nt_lo, 1)
                        v.engine_nop().then_inc(drained[b], 1)

            def pool():
                v.memset(padded[:, :, 0:8], 0.0)
                own.link(v.memset(padded[:, :, 8 + S:16 + S], 0.0))
                hf = xnt.rearrange("p t (k s) -> p t k s", k=KT)
                for g, w in enumerate(WINDOWS):
                    own.wait()
                    for t in range(TB):
                        e = v.tensor_copy(padded[:, :, 8 + t * P:8 + (t + 1) * P], hf[:, t, 2 * g:2 * g + 2, :])
                    own.link(e)
                    own.wait()
                    src, lo, hi = padded, 1, S + 16
                    own.link(v.tensor_tensor(win[0][:, :, 1:hi], src[:, :, 0:hi - 1], src[:, :, 1:hi], ALU.add))
                    for j in range(1, g + 1):
                        m = 1 << (j - 1)
                        src, dst = win[(j - 1) % 2], win[j % 2]
                        lo, hi = lo + m, hi - m
                        own.wait()
                        own.link(v.tensor_tensor(dst[:, :, lo:hi], src[:, :, lo - m:hi - m], src[:, :, lo + m:hi + m],
                                                 ALU.add))
                    own.wait()
                    if g == 0:
                        dve.wait_ge(edge_landed, 16)
                    o = win[g % 2]
                    for side, at in ((0, 8), (1, S)):
                        e = v.tensor_tensor(o[:, :, at:at + 8], o[:, :, at:at + 8],
                                            edge[:, g, side, :].unsqueeze(1).to_broadcast([P, 2, 8]), ALU.mult)
                    own.link(e)
                    own.wait()
                    diff = win[(g + 1) % 2][:, :, 8:8 + S]
                    v.scalar_tensor_tensor(diff, o[:, :, 8:8 + S], 1.0 / w, padded[:, :, 8:8 + S],
                                           ALU.mult, ALU.subtract).then_inc(pool_diff, 1)
                    dve.wait_ge(pool_hi, g + 1)
                    own.link(v.tensor_tensor(ntl[:, 2 * g:2 * g + 2, :], diff, nth[:, 2 * g:2 * g + 2, :].bitcast(F32),
                                             ALU.subtract))
                    v.engine_nop().then_inc(pool_lo, 1)
                    keep_own_chunk(chunk_at(*MOD_POOL[g]))
                split(1)
                n.next(M)
                n.next(T)
                dve.wait_ge(drained[M], n.seen(M))
                dve.wait_ge(drained[T], n.seen(T))
                dve.wait_ge(row_landed, 16)
                own.link(v.tensor_tensor(gate[:, :], gate[:, :], row, ALU.mult))
                own.wait()

            def diff_attention():
                for b in range(6):
                    split(2)
                    n.next(A)
                    o = full_with_piece(B, 2)
                    v.tensor_copy(qkv[:, 1, b * BLK:(b + 1) * BLK], o).then_inc(drained[B], 1)
                dve.wait_ge(attn_landed, 16 * 3)
                l4 = lamrow.rearrange("p (a b j) -> p a b j", a=2, b=2)
                own.link(v.tensor_tensor(lamt.rearrange("p (a j) -> p a j", a=2), l4[:, :, 0, :], l4[:, :, 1, :],
                                         ALU.mult))
                own.wait()
                v.tensor_reduce(lam[:, 0:2], lamt.rearrange("p (a j) -> p a j", a=2), AX.X, ALU.add)\
                 .then_inc(lam_prod, 1)
                dve.wait_ge(lam_exp, 1)
                own.link(v.tensor_tensor(lam[:, 4:5], lam[:, 3:4], lam[:, 2:3], ALU.subtract))
                own.wait()
                own.link(v.tensor_scalar(lam[:, 5:6], lam[:, 4:5], LAM_INIT, None, ALU.subtract))
                own.wait()

                for h in range(H1):
                    for c, b in enumerate((A, B)):
                        o = full(b)
                        if h:
                            dve.wait_ge(drained[B], n.seen(B) - (b == B))
                        v.tensor_reduce(top[:, 2 * c:2 * c + 2], o.rearrange("p (t k) -> p t k", t=TB), AX.X,
                                        ALU.max, negate=True).then_inc(top_ready, 1)
                    dve.wait_ge(drained[A], n.seen(A))
                    dve.wait_ge(drained[B], n.seen(B))
                    own.link(v.reciprocal(inv, total))
                    own.wait()
                    own.link(v.tensor_scalar(invl[:, 0:2], inv[:, 2:4], lam[:, 5:6], None, ALU.mult))
                    own.wait()
                    if h:
                        dve.wait_ge(filled[M], n.seen(M))
                    for t in range(TB):
                        own.link(v.tensor_scalar(av[:, t, :], pr[:, 0, t, :], inv[:, t:t + 1], None, ALU.mult))
                    own.wait()
                    for t in range(TB):
                        v.scalar_tensor_tensor(av[:, t, :], pr[:, 1, t, :], invl[:, t:t + 1], av[:, t, :],
                                               ALU.mult, ALU.add).then_inc(mix_ready, 1)
                    n.next(T)
                    n.next(M)
                dve.wait_ge(heads_rstd, 1)
                for t in range(TB):
                    o = qkv[:, t, 0:D].rearrange("p (h n) -> p h n", h=H1)
                    own.link(v.tensor_tensor(o, o, hss[:, 8 * t:8 * t + 8].unsqueeze(2).to_broadcast([P, H1, P]),
                                             ALU.mult))
                own.wait()
                for t in range(TB):
                    o = qkv[:, t, 0:D].rearrange("p (h n) -> p h n", h=H1)
                    v.scalar_tensor_tensor(o, o, 1.0 - LAM_INIT, subln.unsqueeze(1).to_broadcast([P, H1, P]),
                                           ALU.mult, ALU.mult).then_inc(heads_normed, 1)
                n.next(M)
                n.next(T)
                turned_lo()
                split(4)

            def second_mix():
                o = full(M)
                dve.wait_ge(mix_landed, 16 * 4)
                v.tensor_tensor(gz, o[:, 0:16].rearrange("p (t g) -> p t g", t=TB),
                                gbias.unsqueeze(1).to_broadcast([P, TB, 8]), ALU.add).then_inc(gated, 1)
                v.engine_nop().then_inc(drained[M], 1)
                v.memset(convT[:, :, 0:3], 0.0)
                own.link(v.memset(vbx[:, :, :, P:P + 1], 1.0))
                for b in range(3):
                    split(2)
                    n.next(A)
                    o = full_with_piece(B, 2)
                    v.tensor_copy(qkva[:, 1, b * BLK:(b + 1) * BLK], o).then_inc(drained[B], 1)
                for b in range(2):
                    split(2)
                    n.next(A)
                    o = full_with_piece(B, 2)
                    if b:
                        dve.wait_ge(filled[M], n.seen(M))
                    v.tensor_copy(convin[:, 1, :], o).then_inc(drained[B], 1)
                    v.engine_nop().then_inc(conv_in, 1)
                    dve.wait_ge(conv_in, 2 * b + 2)
                    v.engine_nop().then_inc(drained[A], 1)
                    dve.wait_ge(roped, 4)
                    o = [full(T), full(M)]
                    for q in range(4):
                        k = 4 * b + q
                        pad = convT[:, q % 2, :]
                        own.wait()
                        for t in range(TB):
                            e = v.tensor_copy(pad[:, 3 + t * P:3 + (t + 1) * P], o[t][:, q * P:(q + 1) * P])
                        own.link(e)
                        own.wait()
                        for j in range(4):
                            tap = cols[:, C_CONV + 8 * j + k:C_CONV + 8 * j + k + 1]
                            src = pad[:, j:j + S]
                            if j == 0:
                                own.link(v.tensor_scalar(qkc[:, k, :], src, tap, None, ALU.mult))
                                own.wait()
                            elif j < 3:
                                own.link(v.scalar_tensor_tensor(qkc[:, k, :], src, tap, qkc[:, k, :],
                                                                ALU.mult, ALU.add))
                                own.wait()
                            else:
                                v.scalar_tensor_tensor(qkc[:, k, :], src, tap, qkc[:, k, :], ALU.mult, ALU.add)\
                                 .then_inc(conv_sum, 1)
                        v.engine_nop().then_inc(conv_done, 1)
                    v.engine_nop().then_inc(drained[T], 1)
                    v.engine_nop().then_inc(drained[M], 1)
                split(2)
                n.next(A)
                o = full_with_piece(B, 2)
                v.tensor_copy(vbx[:, 1, :, 0:P], o.rearrange("p (h n) -> p h n", h=HB)).then_inc(drained[B], 1)
                split(2)
                n.next(A)
                n.next(B)
                dve.wait_ge(late_landed, 16)
                dve.wait_ge(drained[A], n.seen(A))
                dve.wait_ge(drained[B], n.seen(B))
                own.link(v.tensor_tensor(obt, obt, convin[:, 0:1, :].to_broadcast([P, TB, 512]), ALU.mult))
                own.wait()
                v.engine_nop().then_inc(ob_scaled, 1)

                dve.wait_ge(mask_landed, 32)
                turned_before = n.seen(M)

                def masked(h):
                    c, p = 2 * (h % 2), pa2[h % 2]
                    if h % 2 == 0:
                        n.next(T)
                    o = full(A)
                    if h >= 2:
                        dve.wait_ge(filled[M], turned_before + h - 1)
                    seg = p.rearrange("p (a k) -> p a k", a=3)
                    osg = o[:, 0:3 * P].rearrange("p (a k) -> p a k", a=3)
                    own.link(v.tensor_tensor(seg[:, 0:3:2, :], osg[:, 0:3:2, :],
                                             mask_q.unsqueeze(1).to_broadcast([P, 2, P]), ALU.add))
                    own.link(v.tensor_copy(seg[:, 1, :], osg[:, 1, :]))
                    own.wait()
                    v.engine_nop().then_inc(drained[A], 1)
                    own.link(v.tensor_reduce(top[:, c:c + 1], p[:, 0:P], AX.X, ALU.max, negate=True))
                    v.tensor_reduce(top[:, c + 1:c + 2], p[:, P:3 * P], AX.X, ALU.max, negate=True)\
                     .then_inc(top_ready, 1)

                def weighted(h):
                    c = 2 * (h % 2)
                    dve.wait_ge(probs_ready, h + 1)
                    own.link(v.reciprocal(inv[:, c:c + 2], total[:, c:c + 2]))
                    own.wait()
                    n.next(M)
                    o = full(B)
                    for t in range(TB):
                        e2 = v.tensor_scalar(qkva[:, t, h * 64:(h + 1) * 64], o[:, t * 64:(t + 1) * 64],
                                             inv[:, c + t:c + t + 1], None, ALU.mult)
                    e2.then_inc(drained[B], 1)

                for h in range(HA + 1):
                    if h < HA:
                        masked(h)
                        split(1)
                    if h:
                        weighted(h - 1)
                split(2)

                v.engine_nop().then_inc(attention_over, 1)
                r0, r1, r2, r3 = va_rows
                o = full(T)
                i_row, f_row = o[0:4, 0:S], o[0:4, S:2 * S]
                dve.wait_ge(rows_act, 1)
                own.link(v.tensor_scalar(r1, f_row, 0.0, None, ALU.min))
                own.wait()
                own.link(v.tensor_tensor(r1, r1, r0, ALU.subtract))
                own.wait()
                own.link(v.tensor_tensor_scan(r2, ones[0:4, 0:1].to_broadcast([4, S]), r1, 0.0, ALU.mult, ALU.add))
                own.wait()
                own.link(v.tensor_tensor(r3, i_row, r2, ALU.subtract))
                own.wait()
                v.engine_nop().then_inc(drained[T], 1)
                own.link(v.tensor_tensor_scan(r0, r3, r3, 0.0, ALU.max, ALU.max))
                own.wait()
                own.link(v.tensor_tensor(r1, r2, r0, ALU.add))
                v.engine_nop().then_inc(rows_step, 1)
                o = full(M)
                v.tensor_copy(agate.rearrange("p g t h -> p (g t h)"), o[:, 0:16]).then_inc(drained[M], 1)
                dve.wait_ge(drained[M], n.seen(M))
                def decays(h):
                    o = full(T)
                    if h:
                        own.wait()
                    for s, (m0, d0) in enumerate(((0, 0), (P, S))):
                        a = agate[:, 0, s, h:h + 1]
                        own.link(v.scalar_tensor_tensor(decay[:, d0:d0 + P], o[:, m0:m0 + P], a, mask_k,
                                                        ALU.subtract, ALU.max))
                    own.link(v.tensor_scalar(decay[:, P:S], o[:, P:S], agate[:, 0, 0, h:h + 1], 0.0,
                                             ALU.subtract, ALU.max))
                    v.engine_nop().then_inc(drained[T], 1)
                    v.engine_nop().then_inc(decay_in, 1)

                for h in range(HB):
                    if h == 0:
                        decays(h)
                    o = full(A)
                    dve.wait_ge(decay_out, h + 1)
                    if h:
                        dve.wait_ge(filled[B], n.seen("small B"))
                    own.link(v.scalar_tensor_tensor(scT, o[:, 0:3 * P], HDB ** -0.5, decay, ALU.mult, ALU.mult))
                    v.engine_nop().then_inc(drained[A], 1)
                    if h + 1 < HB:
                        decays(h + 1)
                    o = full(B)
                    if h:
                        dve.wait_ge(hb_ready, 2 * h)
                    dve.wait_ge(den_abs, h + 1)
                    own.link(v.tensor_tensor(total[:, 0:2], total[:, 0:2], agate[:, 1, :, h], ALU.max))
                    own.wait()
                    for t in range(TB):
                        v.reciprocal(inv[:, t:t + 1], total[:, t:t + 1]).then_inc(den_ready, 1)
                dve.wait_ge(heads_rstd, 2)
                for t in range(TB):
                    o = qkva[:, t, 512:D].rearrange("p (h n) -> p h n", h=HB)
                    own.link(v.tensor_tensor(o, o, hss[:, 4 * t:4 * t + 4].unsqueeze(2).to_broadcast([P, HB, P]),
                                             ALU.mult))
                own.wait()
                own.link(v.tensor_tensor(qkva[:, :, 512:D], qkva[:, :, 512:D], obt, ALU.mult))
                v.engine_nop().then_inc(y_done, 1)
                turned_lo()

                dve.wait_ge(gab_ready, 1)
                for t in range(TB):
                    s = n.next("sums 0") if t == 0 else n.next("sums 1")
                    if t == 0:
                        dve.wait_ge(sums_done, s.at + 1)
                    else:
                        dve.wait_ge(w_used, n.seen("piece") - 1)
                    for c in range(2):
                        own.link(v.tensor_tensor(xnt[:, t, c * BLK:(c + 1) * BLK], ps[:, 2 * t + c, :],
                                                 gab[:, t, c * BLK:(c + 1) * BLK], ALU.mult))
                    v.engine_nop().then_inc(sums_read[t], 1)
                for c in range(2):
                    split(1)
                    sig = gab[:, :, 2 * BLK:3 * BLK] if c == 0 else gab2
                    for t, b in enumerate((A, B)):
                        if t == 0:
                            o = full(A)
                        else:
                            o = full_with_piece(B, 2)
                        own.link(v.tensor_tensor(sig[:, t, :], o, sig[:, t, :], ALU.mult))
                        v.engine_nop().then_inc(drained[b], 1)
                    own.wait()
                    for t in range(TB):
                        own.link(v.tensor_tensor(xnt[:, t, c * BLK:(c + 1) * BLK], xnt[:, t, c * BLK:(c + 1) * BLK],
                                                 sig[:, t, :], ALU.add))
                own.wait()
                for t in range(TB):
                    v.engine_nop().then_inc(merged, 1)
                turned_lo()
                split(4)

            v.engine_nop().then_inc(w_lo, 1)
            o = full(A)
            v.tensor_copy(cols[:, :], o[:, 0:NROWS]).then_inc(cols_copied, 1)
            v.tensor_copy(modb[:, 0:72], o[:, 128:200]).then_inc(cols_copied, 1)
            v.tensor_copy(modb[:, 72:144], o[:, 256:328]).then_inc(cols_copied, 1)
            v.engine_nop().then_inc(drained[A], 1)
            split(2)
            dve.wait_ge(cols_copied, 3)
            dve.wait_ge(cact_ready, 1)
            for j in range(2):
                add_chunk(j + 1)
                keep_own_chunk(chunk_at(*MOD_FIRST[2 * j]))
                keep_chunk(chunk_at(*MOD_FIRST[2 * j + 1]))

            def modulated(layer, j):
                return norm_col(layer, j), mod_cols(layer, 3 * j), mod_cols(layer, 3 * j + 1)

            dve.wait_ge(drained[M], n.seen(M))
            join(*modulated(0, 0), sums=False)
            ffn(0, True)
            join(*modulated(0, 1), split_too=False)
            pool()
            join(*modulated(0, 2))
            ffn(1, True)
            join(*modulated(1, 0))
            ffn(2, True)
            join(*modulated(1, 1))
            diff_attention()
            join(*modulated(1, 2))
            ffn(3, True)
            join(cols[:, C_MIX:C_MIX + KT], final=True)
            second_mix()
            join(cols[:, C_FFN:C_FFN + KT], gated=False)
            ffn(4, False)
            for t in range(TB):
                joined(t, False, 0)
                n.next("x")
                v.engine_nop().then_inc(x_ready, 1)
                r = n.next("rstd")
                if t == 0:
                    dve.wait_ge(row_landed, 48)
                dve.wait_ge(rstd_done, r.at + 1)
                v.scalar_tensor_tensor(xnt[:, t, :], x[:, t, :], rstd[:, t:t + 1], row, ALU.mult, ALU.mult)\
                 .then_inc(y_ready, 1)

        @block.gpsimd
        def _(pool):
            n = Tally()
            own = Chain(pool, pool_chain)
            g = nc.gpsimd

            def load_chunk(layer, chunk):
                c = n.next("chunk")
                src = d["mod_w"][layer].rearrange("(k p) n -> p k n", p=P)
                for h in range(2):
                    if c.i is not None:
                        pool.wait_ge(acc_step, c.at * KT + (4 * h + 4 - KT))
                    pool.dma_start(mraw[h], src[:, 4 * h:4 * h + 4, bass.ds(chunk * MCH, MCH)])\
                        .then_inc(mod_landed[h], 16)

            def load_own_chunk(layer, chunk, h0, used=None, by=(first_used, filled[M])):
                src = d["mod_w"][layer].rearrange("(k p) n -> p k n", p=P)
                for h in range(2):
                    if used is not None:
                        pool.wait_ge(by[h], used[h])
                    pool.dma_start(mfirst[h0 + h], src[:, 4 * h:4 * h + 4, chunk * MCH:(chunk + 1) * MCH])\
                        .then_inc(first_landed[h0 + h], 16)

            def load_chunks(f):
                layer, first, pat, turns = MOD_LOOP[f]
                per = sum(pat)
                if per:
                    with pool.Fori(0, turns) as i:
                        n.enter(i, {"chunk": per})
                        for k in range(per):
                            load_chunk(layer, i * per + (first + k))
                        n.leave(turns)

            def diagonals(layer, v):
                cols_ = mod_cols(layer, v)
                g.tensor_tensor(diag, ident[:, :].unsqueeze(1).to_broadcast([P, KT, P]),
                                cols_.unsqueeze(2).to_broadcast([P, KT, P]), ALU.mult).then_inc(diag_ready, 1)

            def rms(times=1, turn=True):
                for t in range(TB):
                    for _ in range(times):
                        r = n.next("rstd").at
                        pool.wait_ge(sq_done, r + 1)
                        g.tensor_scalar(ss[:, t:t + 1], ss[:, t:t + 1], 1.0 / D, EPS, ALU.mult, ALU.add)\
                         .then_inc(rstd_v, 1)
                        pool.wait_ge(rstd_v, r + 1)
                        g.tensor_tensor(rstd[:, t:t + 1], ss[:, t:t + 1], power[:, 0:1], ALU.pow)\
                         .then_inc(rstd_done, 1)
                    if turn:
                        pool.wait_ge(rstd_done, r + 1)
                        g.tensor_scalar(rdiag[:, t * P:(t + 1) * P], ident[:, :], rstd[:, t:t + 1], None, ALU.mult)\
                         .then_inc(rdiag_ready, 1)

            def pool_signal(s):
                g.engine_nop().then_inc(s, 1)

            def head_rms(k, width):
                own.link(g.tensor_scalar(hss[:, 0:k], hss[:, 0:k], 1.0 / width, EPS, ALU.mult, ALU.add))
                own.wait()
                g.tensor_tensor(hss[:, 0:k], hss[:, 0:k], power[:, 0:1].to_broadcast([P, k]), ALU.pow)\
                 .then_inc(heads_rstd, 1)

            def rope(x1, x2, cos, sin, tmp):
                own.wait()
                g.tensor_tensor(tmp[0], x1, cos, ALU.mult)
                g.tensor_tensor(tmp[1], x2, sin, ALU.mult)
                g.tensor_tensor(tmp[2], x2, cos, ALU.mult)
                own.link(g.tensor_tensor(tmp[3], x1, sin, ALU.mult))
                own.wait()
                g.tensor_tensor(x1, tmp[0], tmp[1], ALU.subtract)
                own.link(g.tensor_tensor(x2, tmp[2], tmp[3], ALU.add))

            def skip(k=1, **kw):
                for name, b in (("a", A), ("b", B), ("t", T), ("m", M)):
                    n.n[b] = n.n.get(b, 0) + kw.get(name, 0) * k

            def ffn(f):
                load_chunks(f)
                skip(a=STEPS, b=STEPS, t=STEPS, m=MOD_LOOP[f][3] * sum(MOD_LOOP[f][2]))

            def join(times=1):
                rms(times)
                skip(a=1, b=1, t=1, m=1)

            def diag_of(layer, v):
                pool.wait_ge(drained[M], n.seen(M))
                diagonals(layer, v)
                skip(t=1, m=1)

            g.memset(power[:, :], -0.5).then_inc(consts_set, 1)
            g.memset(ones[:, :], 1.0).then_inc(consts_set, 1)
            g.memset(small[:, :], 0.0).then_inc(consts_set, 1)
            pool.wait_ge(consts_set, 3)
            for j, (l, c) in enumerate(MOD_FIRST):
                if j % 2 == 0:
                    load_own_chunk(l, c, 0, None if j < 2 else (1, 1))
                else:
                    load_own_chunk(l, c, 2, None if j < 2 else (4, 8), 2 * [acc_step])
            n.n["chunk"] = 2
            pool.wait_ge(first_used, 2)
            pool.wait_ge(filled[M], 4)
            pool.wait_ge(acc_step, 16)
            skip(a=1, m=6)
            join()
            pool.dma_start(row, broadcast(d["pool_scale"], D)).then_inc(row_landed, 16)
            pool.dma_start(edge.rearrange("p g e j -> p (g e j)"), d["edge"]).then_inc(edge_landed, 16)
            ffn(0)
            pool.wait_ge(nt_lo, 4)
            diag_of(0, 2)
            pool.wait_ge(acc_step, KT * n.n["chunk"])
            load_own_chunk(*MOD_POOL[0], 0)
            join()
            for j in range(1, 4):
                load_own_chunk(*MOD_POOL[j], 0, (2 + j, n.n[M] + 2 * j - 1))
            skip(m=8)
            pool.wait_ge(pool_lo, 4)
            diag_of(0, 5)
            join()
            pool.wait_ge(filled[M], n.n[M] - 1)
            ffn(1)
            pool.wait_ge(nt_lo, 8)
            diag_of(0, 8)
            pool.wait_ge(sums_read[0], 2)
            pool.dma_start(subln, broadcast(d["diff_subln_g"], P)).then_inc(attn_landed, 16)
            pool.dma_start(rope1.rearrange("p c t j -> p (c t j)"), d["rope1"]).then_inc(attn_landed, 16)
            pool.dma_start(lamrow, broadcast(d["diff_lambda"].rearrange("a j -> (a j)"), 256)).then_inc(attn_landed, 16)
            join()
            ffn(2)
            pool.wait_ge(nt_lo, 12)
            diag_of(1, 2)
            join()

            skip(a=4, b=4)
            pool.wait_ge(drained[A], n.seen(A))
            pool.wait_ge(drained[B], n.seen(B))
            pool.wait_ge(nt_lo, 16)
            pool.wait_ge(attn_landed, 48)
            for t in range(TB):
                heads = qkv[:, t, 0:2 * D].rearrange("p (h j) -> p h j", j=HD1)
                half = ROT // 2
                c, s = (rope1[:, i, t, :].unsqueeze(1).to_broadcast([P, 4 * H1, half]) for i in range(2))
                tmp = [xn[:, 256 * i:256 * i + 256].rearrange("p (h j) -> p h j", j=half) for i in range(4)]
                rope(heads[:, :, 0:half], heads[:, :, half:ROT], c, s, tmp)
                own.wait()
                pool_signal(roped)
            skip(a=2, b=2)
            skip(H1, a=1, b=1, t=1, m=1)
            diag_of(1, 5)
            pool.wait_ge(out_copied, H1)
            head_rms(2 * H1, P)
            skip(a=1, b=1, t=1, m=1)
            join()
            ffn(3)
            pool.wait_ge(nt_lo, 24)
            diag_of(1, 8)
            pool.wait_ge(drained[M], n.seen(M))
            pool.dma_start(mask_q, d["mask_q"]).then_inc(mask_landed, 16)
            pool.dma_start(mask_k, d["mask_k"]).then_inc(mask_landed, 16)
            pool.dma_start(row, broadcast(d["final_g"], D)).then_inc(row_landed, 16)
            pool.dma_start(w8, d["w_in_2"][0].rearrange("(k p) n -> p k n", p=P)[:, :, GATE_COL:GATE_COL + 8])\
                .then_inc(mix_landed, 16)
            pool.dma_start(gbias[:, 0:4], broadcast(d["b_igate_2"][0], 4)).then_inc(mix_landed, 16)
            pool.dma_start(gbias[:, 4:8], broadcast(d["b_fgate_2"][0], 4)).then_inc(mix_landed, 16)
            pool.dma_start(rope2.rearrange("p c t j -> p (c t j)"), d["rope2"]).then_inc(mix_landed, 16)
            join(2)

            skip(m=1)
            skip(a=2, b=2)
            pool.wait_ge(drained[M], n.seen(M))
            pool.wait_ge(drained[A], n.seen(A))
            pool.wait_ge(drained[B], n.seen(B))
            pool.wait_ge(nt_lo, 28)
            pool.wait_ge(mix_landed, 64)
            for t in range(TB):
                heads = qkva[:, t, 0:1024].rearrange("p (h j) -> p h j", j=HDA)
                half = HDA // 2
                c, s = (rope2[:, i, t, :].unsqueeze(1).to_broadcast([P, 2 * HA, half]) for i in range(2))
                tmp = [xn[:, 512 * i:512 * i + 512].rearrange("p (h j) -> p h j", j=half) for i in range(4)]
                rope(heads[:, :, 0:half], heads[:, :, half:HDA], c, s, tmp)
                own.wait()
                pool_signal(roped)
            pool.wait_ge(conv_done, 8)
            pool.dma_start(convin[:, 0, :], broadcast(d["mlstm_norm_g_2"][0], 512)).then_inc(late_landed, 16)
            skip(a=5, b=5, t=2, m=2)
            skip(HA, a=1, b=1, m=1)
            skip(t=HA // 2)
            pool.wait_ge(attention_over, 1)
            pool.dma_start(pick, d["pick"]).then_inc(late_landed, 16)
            skip(t=1, m=1)
            skip(HB, a=1, b=1, t=1)
            pool.wait_ge(drained[B], n.seen(B))
            head_rms(2 * HB, P)
            join()
            pool.dma_start(row, broadcast(d["norm_final_g_2"], D)).then_inc(row_landed, 16)
            rms(turn=False)


def kernel(**inputs):
    import concourse.bacc as bacc
    from concourse.bass_utils import run_bass_kernel_spmd

    nc = bacc.Bacc("TRN2", target_bir_lowering=False, num_devices=1)
    arrays = {name: np.ascontiguousarray(inputs[name]) for name in INPUTS}
    arrays.update(constants())
    arrays["c_cols"] = np.ascontiguousarray(arrays["c"].reshape(KT, P).T)
    args = {name: nc.dram_tensor(f"in_{name}", a.shape, mybir.dt.from_np(a.dtype), kind="ExternalInput").ap()
            for name, a in arrays.items()}
    out = nc.dram_tensor("out", (1, S, D), F32, kind="ExternalOutput").ap()
    build(nc, args, out)
    result = run_bass_kernel_spmd(nc, [{f"in_{name}": a for name, a in arrays.items()}], core_ids=[0])
    return result.results[0]["out"]
```
